# Optimizing a Trainium2 kernel written in Bass

```python
import jax
import jax.numpy as jnp
from jax import lax
import numpy as np

D_MODEL = 1024
BATCH = 1
SEQ = 512
DEPTH = 2

GRID_W = 64
CTX_LEN = 256
N_MIXERS = 3
N_CONV_LAYERS = (DEPTH + N_MIXERS - 1) // N_MIXERS
N_ATTN_LAYERS = (DEPTH + N_MIXERS - 2) // N_MIXERS
N_LRU_LAYERS = DEPTH // N_MIXERS
N_MOD = 6
EPS = 1e-6

CONV_WIDTH = 31

HEAD_DIM = 64
N_HEADS = D_MODEL // HEAD_DIM
N_KV_HEADS = 4
GQA_GROUP = N_HEADS // N_KV_HEADS
Q_DIM = N_HEADS * HEAD_DIM
KV_DIM = N_KV_HEADS * HEAD_DIM
WINDOW = 128
ATTN_BLOCK = 128
ROPE_BASE = 10000.0
ROPE_PAIRS = HEAD_DIM // 4

D_RNN = D_MODEL
LRU_BLOCKS = 8
LRU_BLOCK_DIM = D_RNN // LRU_BLOCKS
LRU_CONV_W = 4
LRU_C = 8.0

N_EXPERTS = 16
N_GROUPS = 4
EXPERTS_PER_GROUP = N_EXPERTS // N_GROUPS
TOP_K = 2
D_EXPERT = 512
MOE_BLOCK = 128

kernel_name = 'hybrid_conv_swa_rglru_moe_dit'

def rmsnorm(x, g):
    x32 = x.astype(jnp.float32)
    y = x32 * lax.rsqrt(jnp.mean(x32 * x32, axis=-1, keepdims=True) + EPS)
    return (y * g.astype(jnp.float32)).astype(x.dtype)

def layernorm(x, g, b):
    x32 = x.astype(jnp.float32)
    mu = jnp.mean(x32, axis=-1, keepdims=True)
    xc = x32 - mu
    var = jnp.mean(xc * xc, axis=-1, keepdims=True)
    return (xc * lax.rsqrt(var + EPS) * g.astype(jnp.float32) + b.astype(jnp.float32)).astype(x.dtype)

def modulate(h, shift, scale):
    return h * (1.0 + scale) + shift

def depthwise_conv(u, w, b, pad):
    y = lax.conv_general_dilated(u, w[:, None, :].astype(u.dtype), window_strides=(1,), padding=[pad],
                                 dimension_numbers=('NWC', 'WIO', 'NWC'), feature_group_count=u.shape[-1])
    return y + b.astype(u.dtype)

def conformer_conv(h, pw1, pw1_b, dw, dw_b, ln_g, ln_b, pw2, pw2_b):
    u = h @ pw1 + pw1_b
    u = u[..., :D_MODEL] * jax.nn.sigmoid(u[..., D_MODEL:])
    half = (CONV_WIDTH - 1) // 2
    u = depthwise_conv(u, dw, dw_b, (half, half))
    u = jax.nn.silu(layernorm(u, ln_g, ln_b))
    return u @ pw2 + pw2_b

def axial_rope_tables(rows, cols):
    inv = ROPE_BASE ** (-jnp.arange(ROPE_PAIRS, dtype=jnp.float32) / ROPE_PAIRS)
    ar = rows.astype(jnp.float32)[:, None] * inv
    ac = cols.astype(jnp.float32)[:, None] * inv
    ang = jnp.concatenate([ar, ar, ac, ac], axis=-1)
    return jnp.cos(ang), jnp.sin(ang)

def apply_rope(x, cos, sin):
    xr = x.reshape(x.shape[:-1] + (2, 2, ROPE_PAIRS))
    rot = jnp.stack([-xr[..., 1, :], xr[..., 0, :]], axis=-2).reshape(x.shape)
    return x * cos.astype(x.dtype) + rot * sin.astype(x.dtype)

def sink_softmax_av(parts, sink):
    sink_b = sink.astype(jnp.float32).reshape(1, N_KV_HEADS, GQA_GROUP, 1)
    m = sink_b
    for s, _ in parts:
        m = jnp.maximum(m, jnp.max(s, axis=-1))
    den = jnp.exp(sink_b - m)
    out = 0.0
    for s, v in parts:
        p = jnp.exp(s - m[..., None])
        den = den + jnp.sum(p, axis=-1)
        out = out + jnp.einsum('bkgqs,bskd->bqkgd', p, v.astype(jnp.float32))
    return out / jnp.transpose(den, (0, 3, 1, 2))[..., None]

def windowed_sink_gqa(hc, hl, w_qkv, w_o, sink, cos, sin):
    B, S, _ = hl.shape
    L = hc.shape[1]
    nb = S // ATTN_BLOCK
    scale = HEAD_DIM ** -0.5

    def qkv(h):
        t = h @ w_qkv
        n = h.shape[1]
        q = t[..., :Q_DIM].reshape(B, n, N_KV_HEADS, GQA_GROUP, HEAD_DIM) * scale
        k = t[..., Q_DIM:Q_DIM + KV_DIM].reshape(B, n, N_KV_HEADS, HEAD_DIM)
        v = t[..., Q_DIM + KV_DIM:].reshape(B, n, N_KV_HEADS, HEAD_DIM)
        return q, k, v

    qc, kc, vc = qkv(hc)
    ql, kl, vl = qkv(hl)
    ql = apply_rope(ql, cos[None, :, None, None, :], sin[None, :, None, None, :])
    kl = apply_rope(kl, cos[None, :, None, :], sin[None, :, None, :])

    s_cc = jnp.einsum('bqkgd,bckd->bkgqc', qc, kc, preferred_element_type=jnp.float32)
    oc = sink_softmax_av([(s_cc, vc)], sink).reshape(B, L, Q_DIM)

    span = ATTN_BLOCK + 2 * WINDOW
    kp = jnp.pad(kl, ((0, 0), (WINDOW, WINDOW), (0, 0), (0, 0)))
    vp = jnp.pad(vl, ((0, 0), (WINDOW, WINDOW), (0, 0), (0, 0)))
    qb = jnp.swapaxes(ql.reshape(B, nb, ATTN_BLOCK, N_KV_HEADS, GQA_GROUP, HEAD_DIM), 0, 1)
    rel = jnp.arange(ATTN_BLOCK)[:, None] - (jnp.arange(span)[None, :] - WINDOW)
    band = jnp.abs(rel) <= WINDOW

    def block(args):
        j, q = args
        start = j * ATTN_BLOCK
        k = lax.dynamic_slice_in_dim(kp, start, span, axis=1)
        v = lax.dynamic_slice_in_dim(vp, start, span, axis=1)
        kpos = start - WINDOW + jnp.arange(span)
        valid = band & ((kpos >= 0) & (kpos < S))[None, :]
        s_ll = jnp.einsum('bqkgd,bskd->bkgqs', q, k, preferred_element_type=jnp.float32)
        s_ll = jnp.where(valid, s_ll, -jnp.inf)
        s_lc = jnp.einsum('bqkgd,bckd->bkgqc', q, kc, preferred_element_type=jnp.float32)
        return sink_softmax_av([(s_ll, v), (s_lc, vc)], sink)

    ol = lax.map(block, (jnp.arange(nb), qb))
    ol = jnp.swapaxes(ol, 0, 1).reshape(B, S, Q_DIM)
    return oc.astype(hc.dtype) @ w_o, ol.astype(hl.dtype) @ w_o

def _linear_combine(e1, e2):
    a1, b1 = e1
    a2, b2 = e2
    return a1 * a2, a2 * b1 + b2

def rglru_scan(u, wa, ba, wx, bx, lam, h0):
    B, N, _ = u.shape
    ub = u.reshape(B, N, LRU_BLOCKS, LRU_BLOCK_DIM)
    r = jax.nn.sigmoid(jnp.einsum('bnhi,hij->bnhj', ub, wa, preferred_element_type=jnp.float32).reshape(B, N, D_RNN) + ba)
    gi = jax.nn.sigmoid(jnp.einsum('bnhi,hij->bnhj', ub, wx, preferred_element_type=jnp.float32).reshape(B, N, D_RNN) + bx)
    log_a = -LRU_C * jax.nn.softplus(-lam.astype(jnp.float32)) * r
    a = jnp.exp(log_a)
    b = jnp.sqrt(-jnp.expm1(2.0 * log_a)) * (gi * u.astype(jnp.float32))
    b = b.at[:, 0].add(a[:, 0] * h0)
    _, h = lax.associative_scan(_linear_combine, (a, b), axis=1)
    return h, h[:, -1]

def _orient(t, backward):
    return t[:, ::-1] if backward else t

def bidir_rglru(hc, hl, w_in, conv_w, conv_b, wa, ba, wx, bx, lam, w_out):
    def branches(h):
        t = h @ w_in
        return t[..., :D_RNN], jax.nn.gelu(t[..., D_RNN:])

    uc, gc = branches(hc)
    ul, gl = branches(hl)
    B = hl.shape[0]
    yc = jnp.zeros(uc.shape, jnp.float32)
    yl = jnp.zeros(ul.shape, jnp.float32)
    for d in range(2):
        back = d == 1
        pad = (LRU_CONV_W - 1, 0)
        cc = depthwise_conv(_orient(uc, back), conv_w[d], conv_b[d], pad)
        cl = depthwise_conv(_orient(ul, back), conv_w[d], conv_b[d], pad)
        hc_seq, h_ctx = rglru_scan(cc, wa[d], ba[d], wx[d], bx[d], lam[d], jnp.zeros((B, D_RNN), jnp.float32))
        hl_seq, _ = rglru_scan(cl, wa[d], ba[d], wx[d], bx[d], lam[d], h_ctx)
        yc = yc + _orient(hc_seq, back)
        yl = yl + _orient(hl_seq, back)
    oc = (yc * gc.astype(jnp.float32)).astype(hc.dtype) @ w_out
    ol = (yl * gl.astype(jnp.float32)).astype(hl.dtype) @ w_out
    return oc, ol

def route(ht, w_router, router_bias):
    T = ht.shape[0]
    s = jax.nn.sigmoid(jnp.matmul(ht, w_router, preferred_element_type=jnp.float32))
    sel = (s + router_bias.astype(jnp.float32)).reshape(T, N_GROUPS, EXPERTS_PER_GROUP)
    group_score = jnp.sum(lax.top_k(sel, 2)[0], axis=-1)
    grp = jnp.argmax(group_score, axis=-1)
    _, loc = lax.top_k(sel[jnp.arange(T), grp], TOP_K)
    idx = grp[:, None] * EXPERTS_PER_GROUP + loc
    w = jnp.take_along_axis(s, idx, axis=1)
    return idx.astype(jnp.int32), w / jnp.sum(w, axis=-1, keepdims=True)

def moe(h, w_router, router_bias, w1, w3, w2):
    shp = h.shape
    ht = h.reshape(-1, shp[-1])
    T = ht.shape[0]
    idx, gate = route(ht, w_router, router_bias)
    A = T * TOP_K
    flat_e = idx.reshape(-1)
    flat_t = jnp.repeat(jnp.arange(T, dtype=jnp.int32), TOP_K)
    flat_g = gate.reshape(-1)
    order = jnp.argsort(flat_e)
    se = flat_e[order]
    counts = jnp.bincount(flat_e, length=N_EXPERTS)
    padded = (counts + MOE_BLOCK - 1) // MOE_BLOCK * MOE_BLOCK
    pend = jnp.cumsum(padded)
    pstart = pend - padded
    cstart = jnp.cumsum(counts) - counts
    dest = pstart[se] + jnp.arange(A, dtype=jnp.int32) - cstart[se]
    n_slots = -(-A // MOE_BLOCK) * MOE_BLOCK + N_EXPERTS * MOE_BLOCK
    n_blocks = n_slots // MOE_BLOCK
    slot_tok = jnp.zeros((n_slots,), jnp.int32).at[dest].set(flat_t[order])
    slot_gate = jnp.zeros((n_slots,), jnp.float32).at[dest].set(flat_g[order])
    blk_e = jnp.minimum(jnp.searchsorted(pend, jnp.arange(n_blocks, dtype=jnp.int32) * MOE_BLOCK, side='right'),
                        N_EXPERTS - 1)

    def expert_block(args):
        e, tok, g = args
        xb = ht[tok]
        hid = jax.nn.silu(xb @ w1[e]) * (xb @ w3[e])
        return (hid @ w2[e]) * g[:, None].astype(ht.dtype)

    yb = lax.map(expert_block, (blk_e, slot_tok.reshape(n_blocks, MOE_BLOCK), slot_gate.reshape(n_blocks, MOE_BLOCK)))
    out = jnp.zeros_like(ht).at[slot_tok].add(yb.reshape(n_slots, -1))
    return out.reshape(shp)

def setup_inputs(seed: int = 0) -> dict:
    key = jax.random.key(seed)
    keys = iter(jax.random.split(key, 48))

    def nrm(shape, scale):
        return jax.random.normal(next(keys), shape, jnp.float32) * scale

    D = D_MODEL
    nC, nA, nL = N_CONV_LAYERS, N_ATTN_LAYERS, N_LRU_LAYERS
    u = jax.random.uniform(next(keys), (nL, 2, D_RNN), jnp.float32, 0.9, 0.999)
    p = u ** (1.0 / LRU_C)
    return {
        'x': nrm((BATCH, SEQ, D), 1.0),
        'c': nrm((BATCH, D), 1.0),
        'ctx': nrm((BATCH, CTX_LEN, D), 1.0),
        'c_ctx': nrm((D,), 1.0),
        'w_mod': nrm((DEPTH, D, N_MOD * D), 0.5 * D ** -0.5),
        'b_mod': nrm((DEPTH, N_MOD * D), 0.02),
        'norm_mix': 1.0 + nrm((DEPTH, D), 0.02),
        'norm_ffn': 1.0 + nrm((DEPTH, D), 0.02),
        'norm_f': 1.0 + nrm((D,), 0.02),
        'conv_pw1': nrm((nC, D, 2 * D), D ** -0.5),
        'conv_pw1_b': nrm((nC, 2 * D), 0.02),
        'conv_dw': nrm((nC, CONV_WIDTH, D), CONV_WIDTH ** -0.5),
        'conv_dw_b': nrm((nC, D), 0.02),
        'conv_ln_g': 1.0 + nrm((nC, D), 0.02),
        'conv_ln_b': nrm((nC, D), 0.02),
        'conv_pw2': nrm((nC, D, D), D ** -0.5),
        'conv_pw2_b': nrm((nC, D), 0.02),
        'attn_w_qkv': nrm((nA, D, Q_DIM + 2 * KV_DIM), D ** -0.5),
        'attn_w_o': nrm((nA, Q_DIM, D), Q_DIM ** -0.5),
        'attn_sink': nrm((nA, N_HEADS), 0.5),
        'lru_w_in': nrm((nL, D, 2 * D_RNN), D ** -0.5),
        'lru_conv_w': nrm((nL, 2, LRU_CONV_W, D_RNN), LRU_CONV_W ** -0.5),
        'lru_conv_b': nrm((nL, 2, D_RNN), 0.02),
        'lru_wa': nrm((nL, 2, LRU_BLOCKS, LRU_BLOCK_DIM, LRU_BLOCK_DIM), LRU_BLOCK_DIM ** -0.5),
        'lru_ba': nrm((nL, 2, D_RNN), 0.02),
        'lru_wx': nrm((nL, 2, LRU_BLOCKS, LRU_BLOCK_DIM, LRU_BLOCK_DIM), LRU_BLOCK_DIM ** -0.5),
        'lru_bx': nrm((nL, 2, D_RNN), 0.02),
        'lru_lam': jnp.log(p) - jnp.log1p(-p),
        'lru_w_out': nrm((nL, D_RNN, D), D_RNN ** -0.5),
        'moe_w_router': nrm((D, N_EXPERTS), D ** -0.5),
        'moe_router_bias': nrm((N_EXPERTS,), 0.01),
        'moe_w1': nrm((DEPTH, N_EXPERTS, D, D_EXPERT), D ** -0.5),
        'moe_w3': nrm((DEPTH, N_EXPERTS, D, D_EXPERT), D ** -0.5),
        'moe_w2': nrm((DEPTH, N_EXPERTS, D_EXPERT, D), D_EXPERT ** -0.5),
    }

def reference(x, c, ctx, c_ctx, w_mod, b_mod, norm_mix, norm_ffn, norm_f,
              conv_pw1, conv_pw1_b, conv_dw, conv_dw_b, conv_ln_g, conv_ln_b, conv_pw2, conv_pw2_b,
              attn_w_qkv, attn_w_o, attn_sink,
              lru_w_in, lru_conv_w, lru_conv_b, lru_wa, lru_ba, lru_wx, lru_bx, lru_lam, lru_w_out,
              moe_w_router, moe_router_bias, moe_w1, moe_w3, moe_w2):
    B, S, _ = x.shape
    L = ctx.shape[1]
    ROWS = S // GRID_W
    rows = jnp.repeat(jnp.arange(ROWS, dtype=jnp.int32), GRID_W)
    cols = jnp.tile(jnp.arange(GRID_W, dtype=jnp.int32), ROWS)
    cos, sin = axial_rope_tables(rows, cols)
    sc = jax.nn.silu(c)
    scc = jax.nn.silu(c_ctx)
    xl, xc = x, ctx
    for i in range(DEPTH):
        last = i == DEPTH - 1
        kind, slot = i % N_MIXERS, i // N_MIXERS
        mod_l = jnp.split((sc @ w_mod[i] + b_mod[i])[:, None, :], N_MOD, axis=-1)
        mod_c = jnp.split(scc @ w_mod[i] + b_mod[i], N_MOD, axis=-1)
        hl = modulate(rmsnorm(xl, norm_mix[i]), mod_l[0], mod_l[1])
        hc = None if (last and kind == 0) else modulate(rmsnorm(xc, norm_mix[i]), mod_c[0], mod_c[1])
        if kind == 0:
            prm = (conv_pw1[slot], conv_pw1_b[slot], conv_dw[slot], conv_dw_b[slot],
                   conv_ln_g[slot], conv_ln_b[slot], conv_pw2[slot], conv_pw2_b[slot])
            yl = conformer_conv(hl, *prm)
            yc = None if last else conformer_conv(hc, *prm)
        elif kind == 1:
            yc, yl = windowed_sink_gqa(hc, hl, attn_w_qkv[slot], attn_w_o[slot], attn_sink[slot], cos, sin)
        else:
            yc, yl = bidir_rglru(hc, hl, lru_w_in[slot], lru_conv_w[slot], lru_conv_b[slot], lru_wa[slot],
                                 lru_ba[slot], lru_wx[slot], lru_bx[slot], lru_lam[slot], lru_w_out[slot])
        xl = xl + mod_l[2] * yl
        moe_prm = (moe_w_router, moe_router_bias, moe_w1[i], moe_w3[i], moe_w2[i])
        hl2 = modulate(rmsnorm(xl, norm_ffn[i]), mod_l[3], mod_l[4])
        if last:
            xl = xl + mod_l[5] * moe(hl2, *moe_prm)
        else:
            xc = xc + mod_c[2] * yc
            hc2 = modulate(rmsnorm(xc, norm_ffn[i]), mod_c[3], mod_c[4])
            y2 = moe(jnp.concatenate([hc2, hl2], axis=1), *moe_prm)
            xc = xc + mod_c[5] * y2[:, :L]
            xl = xl + mod_l[5] * y2[:, L:]
    return rmsnorm(xl, norm_f)


_drawn_inputs = setup_inputs


def setup_inputs(seed=0):
    import zlib

    import numpy as np

    out = dict(_drawn_inputs(seed))
    spreads = {}
    factors = {'norm_mix': 2.786,
     'norm_f': 8.132,
     'conv_pw1_b': 3.691,
     'conv_ln_g': 2.721,
     'conv_ln_b': 3.504,
     'attn_sink': 64.0}
    for name, (base, spread) in spreads.items():
        noise = np.random.default_rng([zlib.crc32(name.encode()), seed]).standard_normal(out[name].shape)
        drawn = base * np.exp(spread * noise) if base else spread * noise
        out[name] = jnp.asarray(drawn.astype(out[name].dtype))
    for name, factor in factors.items():
        out[name] = (out[name] * factor).astype(out[name].dtype)
    return out
```

```python
from contextlib import ExitStack

import numpy as np

import concourse.bass as bass
from concourse import mybir

ALU = mybir.AluOpType
ACT = mybir.ActivationFunctionType
AX = mybir.AxisListType
F32 = mybir.dt.float32
I32 = mybir.dt.int32
U32 = mybir.dt.uint32

P = 128
D = 1024
KT = D // P
SEQ = 512
CTX = 256
CT = CTX // P
LT = SEQ // P
TILES = CT + LT
TOK = TILES * P
NMOD = 6
MCOLS = NMOD * KT
EPS = 1e-6
TAPS = 31
HALF = TAPS // 2
PADW = HALF + CTX + HALF + SEQ + HALF
CONVW = CTX + HALF + SEQ
LAT0 = CTX + HALF
NH = 16
DH = 64
NKV = 4
GQ = NH // NKV
NE = 16
NG = 4
FE = 512
MAXB = [TILES * 2 + NE, LT * 2 + NE]
GRID_W = 64
PAIRS = DH // 4
BIG = 1e30

CW = {}
_at = 0
for _n, _w in (("ident", P), ("tri", P), ("pick", 2), ("tokid", TILES), ("rev4", NG), ("rev16", NE), ("iota", MAXB[0]),
               ("thr", TILES), ("mask_mid", 5 * P), ("mask_first", 4 * P), ("cos", LT * DH), ("sin", LT * DH)):
    if _n == "mask_mid":
        EARLY_W = _at
    CW[_n] = (_at, _w)
    _at += _w
CONSTS_W = _at


def constant_table():
    t = np.zeros((P, CONSTS_W), np.float32)

    def put(name, a):
        at, w = CW[name]
        t[:, at:at + w] = a

    i = np.arange(P)
    put("ident", np.eye(P))
    put("tri", i[:, None] < i[None, :])
    put("pick", i[:, None] % (P // 4) == np.arange(2)[None, :])
    put("tokid", i[:, None] + P * np.arange(TILES)[None, :])
    put("rev4", NG - np.arange(NG)[None, :])
    put("rev16", NE - np.arange(NE)[None, :])
    put("iota", np.arange(MAXB[0])[None, :])
    put("thr", P * np.arange(TILES)[None, :])
    low = np.where(i[None, :] >= i[:, None], 0.0, -BIG)
    up = np.where(i[None, :] <= i[:, None], 0.0, -BIG)
    nil = np.zeros((P, P))
    put("mask_mid", np.concatenate([nil, nil, low, nil, up], 1))
    put("mask_first", np.concatenate([nil, nil, nil, up], 1))
    inv = np.float32(10000.0) ** (-np.arange(PAIRS, dtype=np.float32) / np.float32(PAIRS))
    tok = np.arange(SEQ)
    ar = (tok // GRID_W).astype(np.float32)[:, None] * inv
    ac = (tok % GRID_W).astype(np.float32)[:, None] * inv
    ang = np.concatenate([ar, ar, ac, ac], -1).astype(np.float32)
    sign = np.concatenate([-np.ones(PAIRS), np.ones(PAIRS)] * 2).astype(np.float32)
    put("cos", np.cos(ang).reshape(LT, P, DH).transpose(1, 0, 2).reshape(P, -1))
    put("sin", (np.sin(ang) * sign).reshape(LT, P, DH).transpose(1, 0, 2).reshape(P, -1))
    return t


VECS = (("norm_mix", 2 * KT), ("norm_ffn", 2 * KT), ("conv_pw1_b", 2 * KT), ("conv_dw_b", KT),
        ("conv_ln_g", KT), ("conv_ln_b", KT), ("c", KT), ("c_ctx", KT))


class Steps:

    def __init__(self, eng, sem, n=0):
        self.eng, self.sem, self.n = eng, sem, n

    def __call__(self, ins):
        self.n += 1
        ins.then_inc(self.sem, 1)
        self.eng.wait_ge(self.sem, self.n)


def build(nc, a, out):
    with ExitStack() as stack:
        def sb(name, shape, dt=F32):
            return stack.enter_context(nc.sbuf_tensor(name, shape, dt))

        def sem(name):
            return stack.enter_context(nc.semaphore(name))

        def dram(name, shape, dt=F32):
            return nc.dram_tensor(name, shape, dt, kind="Internal").ap()

        X = sb("X", [P, TILES, D])
        HT = sb("HT", [P, KT, TOK])
        RING = sb("RING", [P, 6, 4096])
        ROWS = sb("ROWS", [P, 6, D])
        AR = sb("AR", [P, 8192])
        CN = sb("CN", [P, EARLY_W])
        ones = sb("ones", [P, P])
        vrow = ROWS[:, 0, 0:4 * P].rearrange("p (a n) -> p a n", a=4)
        cols = sb("cols", [P, 96 + 88 + TAPS * KT])
        sc2 = sb("sc2", [P, KT, P // 4])
        sgc = sb("sgc", [P, 2 * KT])
        modc = sb("modc", [P, 2, 2, MCOLS])
        ss = sb("ss", [P, TILES])
        rstd = sb("rstd", [P, TILES])
        WRT = sb("WRT", [P, KT, NE])
        rbias = sb("rbias", [P, NE])
        E16 = sb("E16", [P, 4, NE])
        GATE = sb("GATE", [P, 2, TILES])
        DST = sb("DST", [P, 2, TILES], U32)
        IDX = sb("IDX", [P, MAXB[0] + 1], U32)
        INFO = sb("INFO", [P, MAXB[0] + 3], I32)
        icur = sb("icur", [P, 1], U32)
        sinkb = sb("sinkb", [P, NH])
        mx = sb("mx", [P, LT * NH])
        nmx = sb("nmx", [P, LT * NH])
        rsum = sb("rsum", [P, LT * NH])
        esk = sb("esk", [P, 2, NH])
        PS = stack.enter_context(nc.psum_tensor("PS", [P, 8, 512], F32))
        PSF = PS[:, :, :].rearrange("p b n -> p (b n)")

        at = [2 * D]

        def table(a_, b_):
            at[0] += a_ * b_
            return RING[:, 0, at[0] - a_ * b_:at[0]].rearrange("p (a b) -> p a b", a=a_)

        SIG, SEL, OH1, OH2 = (table(TILES, NE) for _ in range(4))
        TMP = table(MAXB[0], NE)
        G4 = table(6, TILES * NG)
        S6 = table(8, TILES)
        BLK = table(1, MAXB[0])[:, 0, :]
        slrow = table(1, P)[:, 0, :]
        zeros = AR[:, 7 * D:7 * D + P]

        rowsd = [dram(f"rows_of_layer{L}", [2 * NMOD, D]) for L in range(2)]
        h2d = [dram(f"moe_in{L}", [TOK, D]) for L in range(2)]
        slotd = [dram(f"slot_token{L}", [(MAXB[L] + 1) * P, 1]) for L in range(2)]
        yd = [dram(f"moe_out{L}", [(MAXB[L] + 1) * P, D]) for L in range(2)]

        def const(name, parts=P):
            at, w = CW[name]
            if at >= EARLY_W:
                return AR[:, 3 * D + at - EARLY_W:3 * D + at - EARLY_W + w]
            return CN[0:parts, at:at + w]

        ident = const("ident")
        tri = const("tri")

        BM = 0
        VC = {}
        at = 2 * MCOLS
        for n, w in VECS:
            VC[n] = at
            at += w
        DW = at

        def ar(at, shape):
            n = int(np.prod(shape))
            v = AR[:, at:at + n]
            if len(shape) == 2:
                v = v.rearrange("p (a b) -> p a b", a=shape[0])
            if len(shape) == 3:
                v = v.rearrange("p (a b c) -> p a b c", a=shape[0], b=shape[1])
            return v

        def slot(i, k):
            return RING[:, i, :].rearrange("p (k n) -> p k n", k=k)

        def bc(ap, shape):
            return ap.to_broadcast([P] + list(shape))

        def stream(t):
            return 0 if t < CT else 1

        x_in = sem("x_in")
        par_in = sem("par_in")
        zero_out = [sem(f"zero_out{L}") for L in range(2)]
        dve_step = sem("dve_step")
        act_step = sem("act_step")
        ones_set = sem("ones_set")
        par_turned = sem("par_turned")
        par_cols = sem("par_cols")
        sg_done = sem("sg_done")
        sc_ready = sem("sc_ready")
        modA_in = [sem(f"modA_in{i}") for i in range(4)]
        modB_in = [sem(f"modB_in{i}") for i in range(5)]
        part_summed = sem("mod_part_summed")
        part_copied = sem("mod_part_copied")
        part_turned = sem("mod_part_turned")
        mod_summed = [sem(f"mod_summed{L}") for L in range(2)]
        mod_cols = [sem(f"mod_cols{L}") for L in range(2)]
        mod_turned = [sem(f"mod_turned{L}") for L in range(2)]
        mod_rows = [sem(f"mod_rows{L}") for L in range(2)]
        rows_out = [sem(f"rows_out{L}") for L in range(2)]
        rows_in = [sem(f"rows_in{L}") for L in range(2)]
        gates_in = [sem(f"gates_in{L}") for L in range(2)]
        sq_done = [sem("sq_done")] * 2
        ms_ready = [sem("ms_ready")] * 2
        rms_ready = [sem("rms_ready")] * 2
        xn_ready = [sem("xn_ready")] * 2
        xn_turned = [sem("xn_turned")] * 2
        hA_ready = [sem("hA_ready")] * 2
        hB_ready = [sem("hB_ready")] * 2
        before_mixer = [sq_done[0], ms_ready[0], rms_ready[0], xn_ready[0], xn_turned[0], hA_ready[0], hB_ready[0]]
        pw_in = [sem(f"pw_in{j}") for j in range(2)]
        gate_summed = [sem(f"gate_summed{j}") for j in range(2)]
        val_summed = [sem(f"val_summed{j}") for j in range(2)]
        sig_done = [sem(f"sig_done{j}") for j in range(2)]
        glu_done = [sem(f"glu_done{j}") for j in range(2)]
        conv_step = sem("conv_step")
        conv_done = sem("conv_done")
        pad_zero = sem("pad_zero")
        mean_summed = sem("mean_summed")
        centred = sem("centred")
        squared = sem("squared")
        sq_used = sem("sq_used")
        var_summed = sem("var_summed")
        var_ready = sem("var_ready")
        std_ready = sem("std_ready")
        scaled = sem("scaled")
        z_ready = sem("z_ready")
        w_in = [sem(f"proj_w_in{L}") for L in range(2)]
        brow_in = sem("brow_in")
        again = []

        def both(name):
            again.append(sem(name))
            return [again[-1]] * 2

        y_summed = both("y_summed")
        y_used = both("y_used")
        x_new = both("x_new")
        f_sq = both("f_sq")
        f_ms = both("f_ms")
        f_rms = both("f_rms")
        h2_ready = both("h2_ready")
        h2_out = [[both(f"h2_out{i}")[0] for i in range(2)]] * 2
        h2_turned = both("h2_turned")
        h2A = both("h2A_ready")
        h2B = both("h2B_ready")
        logits = both("logits")
        sig_ready = both("sig_ready")
        chosen = both("chosen")
        ranked = both("ranked")
        dest_ready = both("dest_ready")
        scattered = [sem(f"scattered{L}") for L in range(2)]
        slots_in = both("slots_in")
        slots_turned = both("slots_turned")
        idx_ready = both("idx_ready")
        w1_in = both("w1_in")
        w3_in = both("w3_in")
        w2_in = both("w2_in")
        w13_used = both("w13_used")
        w2_used = both("w2_used")
        idx_set = both("idx_set")
        idx_first = both("idx_first")
        xg_in = [sem(f"xg_in{L}") for L in range(2)]
        xg_turned = both("xg_turned")
        xTa = both("xTa_ready")
        xTb = both("xTb_ready")
        up1_done = both("up1_done")
        silu_done = both("silu_done")
        hid_ready = both("hid_ready")
        hid_turned = both("hid_turned")
        hT_ready = both("hT_ready")
        ya_ready = both("ya_ready")
        yb_ready = both("yb_ready")
        y_out = both("y_out")
        nil_set = both("nil_set")
        nil_out = both("nil_out")
        c1_in = [[sem(f"choice1_in{L}{i}") for i in range(2)] for L in range(2)]
        c2_in = [[sem(f"choice2_in{L}{i}") for i in range(2)] for L in range(2)]
        mixed = both("mixed")
        x_done = both("x_done")
        wqkv_in = [sem(f"wqkv_in{i}") for i in range(3)]
        tables_in = sem("tables_in")
        qkv_summed = sem("qkv_summed")
        qkv_tok = sem("qkv_tok")
        roped = sem("roped")
        q_turned = sem("q_turned")
        qA_ready = sem("qA_ready")
        qB_ready = sem("qB_ready")
        k_ready = sem("k_ready")
        v_ready = sem("v_ready")
        scored = sem("scored")
        s_masked = sem("s_masked")
        neg_ready = sem("neg_ready")
        exp_done = sem("exp_done")
        p_turned = sem("p_turned")
        pA_ready = sem("pA_ready")
        pB_ready = sem("pB_ready")
        av_done = sem("av_done")
        sinkd = sem("sink_minus_max")
        sinke = sem("sink_exp")
        o_ready = sem("o_ready")
        o_turned = sem("o_turned")
        oA_ready = sem("oA_ready")
        oB_ready = sem("oB_ready")
        fin_ready = sem("fin_ready")
        out_sem = sem("out_sem")

        dve_n = [0]
        act_n = [0]

        def mod_sum(L, at, w=1):
            return PS[:, 7, bass.ds(at * 2 + L * 2 * MCOLS, 2 * w)]

        PARTS = ROWS[:, 0:3, :].rearrange("p a n -> p (a n)")[:, 0:2560].rearrange("p (c n) -> p c n", c=5)

        MODT = ROWS[0:2 * MCOLS, 2, 512:512 + 2 * P].rearrange("p (l n) -> p l n", l=2)

        def mod_rows_sum(pe, bank, w):
            for k in range(KT):
                g = 32 * (k % 4)
                ins = pe.matmul(PS[g:g + 32, bank, :], sc2[:, k, :], w[:, k, :], start=(k < 4), stop=(k >= 4),
                                tile_position=(0, g))
            ins.then_inc(part_summed, 1)

        def mod_rows_add(pe, L, at, c):
            for g in range(4):
                ins = pe.matmul(mod_sum(L, at + g), PARTS[:, c, g * P:(g + 1) * P], const("pick"), start=True, stop=True)
            ins.then_inc(part_turned, 1)

        def mod_columns(dve, L, v0, v1):
            st = Steps(dve, dve_step, dve_n[0])
            c0, c1 = v0 * KT, v1 * KT
            pm = mod_sum(L, c0, c1 - c0).rearrange("p (m s) -> p m s", s=2)
            for s in range(2):
                st(nc.vector.tensor_tensor(modc[:, L, s, c0:c1], pm[:, :, s],
                                           cols[:, BM + L * MCOLS + c0:BM + L * MCOLS + c1], ALU.add))
            for s in range(2):
                for v, n in ((1, "norm_mix"), (4, "norm_ffn")):
                    if not v0 <= v < v1:
                        continue
                    c = modc[:, L, s, v * KT:(v + 1) * KT]
                    g = cols[:, VC[n] + L * KT:VC[n] + (L + 1) * KT]
                    st(nc.vector.scalar_tensor_tensor(out=c, in0=c, scalar=1.0, in1=g, op0=ALU.add, op1=ALU.mult))
            nc.vector.engine_nop().then_inc(mod_cols[L], 1)
            dve_n[0] = st.n

        def mod_rows_turn(pe, L):
            pe.wait_ge(mod_cols[L], 2 - L)
            pe.transpose(PS[0:2 * MCOLS, 4 + L, 0:P], modc[:, L, :, :].rearrange("p s m -> p (s m)"), ident).then_inc(mod_turned[L], 1)

        def mod_rows_copy(dve, L):
            dve.wait_ge(mod_turned[L], 1)
            nc.vector.tensor_copy(MODT[:, L, :], PS[0:2 * MCOLS, 4 + L, 0:P]).then_inc(mod_rows[L], 1)

        def mod_rows_store(eng, L):
            eng.wait_ge(mod_rows[L], 1)
            eng.dma_start(rowsd[L].rearrange("v (k p) -> (v k) p", p=P), MODT[:, L, :]).then_inc(rows_out[L], 16)

        def load_row(eng, L, s, v, where, done):
            eng.dma_start(ROWS[:, where, :], rowsd[L][s * NMOD + v, :].partition_broadcast(P)).then_inc(done, 16)

        XN = ar(0, [2, D])
        JUNK = ar(2 * D, [D])
        CG = ar(3 * D, [4, D])

        def norm_act(act, L, first_wait, raw=False):
            st = Steps(act, act_step, act_n[0])
            for t in range(TILES):
                first_wait(act, t)
                if t:
                    act.wait_ge(sq_done[L], t)
                nc.scalar.activation(JUNK, X[:, t, :], ACT.Square, accum_out=ss[:, t:t + 1]).then_inc(sq_done[L], 1)
            act.wait_ge(ms_ready[L], 1)
            nc.scalar.activation(rstd[:, :], ss[:, :], ACT.Sqrt).then_inc(rms_ready[L], 1)
            for t in range(TILES):
                s = stream(t)
                act.wait_ge(xn_turned[L], t + 1)
                if raw:
                    nc.scalar.activation(HT[:, 0:4, t * P:(t + 1) * P],
                                         PS[:, 4 * (t % 2), :].rearrange("p (k n) -> p k n", k=4),
                                         ACT.Copy).then_inc(hA_ready[L], 1)
                    continue
                for k in range(KT // 2):
                    ins = nc.scalar.activation(HT[:, k, t * P:(t + 1) * P], PS[:, 4 * (t % 2), k * P:(k + 1) * P],
                                               ACT.Identity, scale=modc[:, L, s, KT + k:KT + k + 1],
                                               bias=modc[:, L, s, k:k + 1])
                ins.then_inc(hA_ready[L], 1)
            act_n[0] = st.n

        def norm_dve(dve, L, raw=False):
            st = Steps(dve, dve_step, dve_n[0])
            dve.wait_ge(sq_done[L], TILES)
            nc.vector.tensor_scalar(ss[:, :], ss[:, :], 1.0 / D, EPS, ALU.mult, ALU.add).then_inc(ms_ready[L], 1)
            dve.wait_ge(rms_ready[L], 1)
            st(nc.vector.reciprocal(rstd[:, :], rstd[:, :]))
            for t in range(TILES + 1):
                if t < TILES:
                    if t >= 2:
                        dve.wait_ge(xn_turned[L], t - 1)
                    nc.vector.tensor_scalar(XN[:, t % 2, :], X[:, t, :], rstd[:, t:t + 1], None,
                                            ALU.mult).then_inc(xn_ready[L], 1)
                if t >= 1:
                    u, s = t - 1, stream(t - 1)
                    dve.wait_ge(xn_turned[L], u + 1)
                    if raw:
                        nc.vector.tensor_copy(HT[:, 4:8, u * P:(u + 1) * P],
                                              PS[:, 4 * (u % 2) + 1, :].rearrange("p (k n) -> p k n", k=4)).then_inc(
                                                  hB_ready[L], 1)
                        continue
                    for k in range(KT // 2, KT):
                        kk = k - KT // 2
                        ins = nc.vector.tensor_scalar(HT[:, k, u * P:(u + 1) * P],
                                                      PS[:, 4 * (u % 2) + 1, kk * P:(kk + 1) * P],
                                                      modc[:, L, s, KT + k:KT + k + 1], modc[:, L, s, k:k + 1],
                                                      ALU.mult, ALU.add)
                    ins.then_inc(hB_ready[L], 1)
            dve_n[0] = st.n

        def norm_pe(pe, L):
            for t in range(TILES):
                pe.wait_ge(xn_ready[L], t + 1)
                if t >= 2:
                    pe.wait_ge(hA_ready[L], t - 1)
                    pe.wait_ge(hB_ready[L], t - 1)
                for k in range(KT):
                    ins = pe.transpose(PS[:, 4 * (t % 2) + k // 4, (k % 4) * P:(k % 4 + 1) * P],
                                       XN[:, t % 2, k * P:(k + 1) * P], ident)
                ins.then_inc(xn_turned[L], 1)

        MOD_BANKS = (2, 3, 6, 2)
        PWB = RING[:, 0, :].rearrange("p (j u k n) -> p j u k n", j=2, u=2, k=KT)

        def load_pw(sp, i, js=range(2)):
            pw = a["conv_pw1"][0].rearrange("(k p) n -> p k n", p=P)
            for j in js:
                for u in range(2):
                    at = i * 2 * P + (j * P + (1 - u) * D)
                    sp.dma_start(PWB[:, j, u, :, :], pw[:, :, bass.ds(at, P)]).then_inc(pw_in[j], 16)

        with nc.Block() as block:
            @block.sync
            def _(sp):
                sp.dma_start(CN[:, :], a["consts"][:, 0:EARLY_W]).then_inc(par_in, 16)
                for L in range(2):
                    sp.dma_start(vrow[L * MCOLS:(L + 1) * MCOLS, 0, :],
                                 a["b_mod"][L].rearrange("(r q) -> r q", q=P)).then_inc(par_in, 16)
                at = 0
                for n, w in VECS:
                    src = a[n]
                    src = src.rearrange("(r q) -> r q", q=P) if len(src.shape) == 1 else \
                        src.rearrange("l (r q) -> (l r) q", q=P)
                    sp.dma_start(vrow[at:at + w, 1, :], src).then_inc(par_in, 16)
                    at += w
                dw = a["conv_dw"][0].rearrange("t (r q) -> (t r) q", q=P)
                for i in range(2):
                    n = TAPS * KT // 2
                    sp.dma_start(vrow[0:n, 2 + i, :], dw[i * n:(i + 1) * n, :]).then_inc(par_in, 16)
                wm = a["w_mod"][0].rearrange("(k p) n -> p k n", p=P)
                for c in range(4):
                    sp.dma_start(slot(1 + c, KT), wm[:, :, c * 512:(c + 1) * 512]).then_inc(modA_in[c], 16)
                load_pw(sp, 0)

            @block.scalar
            def _(act):
                act.dma_start(X[:, 0:CT, :], a["ctx"][0].rearrange("(t p) d -> p t d", p=P)).then_inc(x_in, 16)
                act.dma_start(X[:, CT:TILES, :], a["x"][0].rearrange("(t p) d -> p t d", p=P)).then_inc(x_in, 16)
                act.dma_start(WRT[:, :, :], a["moe_w_router"].rearrange("(k p) e -> p k e", p=P)).then_inc(par_in, 16)
                act.dma_start(rbias[:, :], a["moe_router_bias"].partition_broadcast(P)).then_inc(par_in, 16)
                act.dma_start(sinkb[:, :], a["attn_sink"][0].partition_broadcast(P)).then_inc(par_in, 16)
                act.wait_ge(par_cols, 2)
                nc.scalar.activation(sgc[:, :], cols[:, VC["c"]:VC["c"] + 2 * KT], ACT.Sigmoid).then_inc(sg_done, 1)
                norm_act(act, 0, lambda e, t: e.wait_ge(x_in, 32) if t == 0 else None, raw=True)
                for c in range(4):
                    act.wait_ge(part_summed, c + 1)
                    nc.scalar.activation(PARTS[:, c, :], PS[:, MOD_BANKS[c], :], ACT.Copy).then_inc(part_copied, 1)
                act.wait_ge(hA_ready[0], TILES)
                act.wait_ge(mod_cols[0], 1)
                for k in range(KT // 2):
                    for s, (t0, t1) in enumerate(((0, CTX), (CTX, TOK))):
                        nc.scalar.activation(HT[:, k, t0:t1], HT[:, k, t0:t1], ACT.Identity,
                                             scale=modc[:, 0, s, KT + k:KT + k + 1], bias=modc[:, 0, s, k:k + 1])

            @block.gpsimd
            def _(pool):
                pool.memset(ones[:, :], 1.0).then_inc(ones_set, 1)
                pool.memset(zeros, 0.0).then_inc(ones_set, 1)
                pool.wait_ge(ones_set, 2)
                for L in range(2):
                    pool.dma_start(slotd[L].rearrange("(b p) o -> b (p o)", p=P),
                                   zeros[0:MAXB[L] + 1, :]).then_inc(zero_out[L], 16)
                for L in range(2):
                    pool.wait_ge(zero_out[L], 16)

            n_par = 1 + 2 + len(VECS) + 2 + 3

            @block.tensor
            def _(pe):
                pe.wait_ge(par_in, 16 * n_par)
                n = TAPS * KT // 2
                pe.transpose(PS[:, 0, 0:2 * MCOLS], vrow[0:2 * MCOLS, 0, :], CN[0:2 * MCOLS, 0:2 * MCOLS])
                pe.transpose(PS[:, 0, 96:184], vrow[0:88, 1, :], CN[0:88, 0:88])
                for i in range(2):
                    ins = pe.transpose(PS[:, 0, 184 + i * n:184 + (i + 1) * n], vrow[0:n, 2 + i, :], CN[0:n, 0:n])
                ins.then_inc(par_turned, 1)
                pe.wait_ge(sc_ready, 1)

                def add(c):
                    pe.wait_ge(part_copied, c + 1)
                    mod_rows_add(pe, 0, 4 * c, c)

                pe.wait_ge(modA_in[0], 16)
                mod_rows_sum(pe, MOD_BANKS[0], slot(1, KT))
                norm_pe(pe, 0)
                for c in range(1, 4):
                    pe.wait_ge(modA_in[c], 16)
                    if c == 3:
                        pe.wait_ge(part_copied, 1)
                    mod_rows_sum(pe, MOD_BANKS[c], slot(1 + c, KT))
                    add(c - 1)
                add(3)
                pe.wait_ge(part_turned, 4)
                pe.sem_inc(part_turned, 1)
                pe.sem_inc(mod_summed[0], 1)

            @block.vector
            def _(dve):
                nc.vector.memset(sc2[:, :, :], 0.0).then_inc(par_cols, 1)
                dve.wait_ge(par_turned, 1)
                nc.vector.tensor_copy(cols[:, :], PS[:, 0, 0:184 + TAPS * KT]).then_inc(par_cols, 1)
                dve.wait_ge(par_cols, 2)
                dve.wait_ge(sg_done, 1)
                for s, n in ((1, "c"), (0, "c_ctx")):
                    at = VC[n] - VC["c"]
                    ins = nc.vector.tensor_tensor(sc2[:, :, s], cols[:, VC[n]:VC[n] + KT], sgc[:, at:at + KT], ALU.mult)
                ins.then_inc(sc_ready, 1)
                norm_dve(dve, 0, raw=True)
                dve.wait_ge(mod_summed[0], 1)
                mod_columns(dve, 0, 0, 2)
                dve.wait_ge(mod_cols[0], 1)
                dve.wait_ge(hB_ready[0], TILES)
                for k in range(KT // 2, KT):
                    for s, (t0, t1) in enumerate(((0, CTX), (CTX, TOK))):
                        nc.vector.tensor_scalar(HT[:, k, t0:t1], HT[:, k, t0:t1], modc[:, 0, s, KT + k:KT + k + 1],
                                                modc[:, 0, s, k:k + 1], ALU.mult, ALU.add)

        V = ar(0, [KT, CONVW])
        UP = ar(KT * CONVW, [2, PADW])
        ACC2 = ROWS[:, 3, 0:CONVW]
        SGT = ROWS[:, 4:6, 0:TOK]
        SQ = ar(KT * CONVW, [2, CONVW])
        Wpw2 = [slot(4, 4), slot(5, 4)]
        BROW = RING[:, 0, 0:D]
        JUNK2 = RING[:, 0, D:2 * D]
        STD = ROWS[:, 3, 0:CONVW]
        MEAN = PSF[:, 0:CONVW]
        VAR = PSF[:, 1024:1024 + CONVW]
        NSTEP = 2 * (1 + TAPS)
        MODS = [(0, 2 * KT + 4 * c, 2) for c in range(2)] + [(1, 4 * c, 3) for c in range(3)]
        segs = ((0, 0, CTX, HALF), (CTX, 1, SEQ, HALF + CTX + HALF))

        def conv_bank(j, u, lat):
            return PS[:, 3 * j + u, 0:SEQ] if lat else PS[:, 3 * j + 2, u * CTX:(u + 1) * CTX]

        with nc.Block() as block:
            @block.sync
            def _(sp):
                wm = [a["w_mod"][L].rearrange("(k p) n -> p k n", p=P) for L in range(2)]
                for one in before_mixer:
                    sp.sem_clear(one)
                def pair(i, more):
                    for c, (L, at, n) in enumerate(MODS):
                        sp.wait_ge(part_turned, i * 5 + (1 + c))
                        sp.dma_start(slot(1 + c, KT),
                                     wm[L][:, :, bass.ds(i * n * 512 + at * P, 512)]).then_inc(modB_in[c], 16)
                        if more and c in (1, 4):
                            j = c // 4
                            sp.wait_ge(val_summed[j], i + 1)
                            load_pw(sp, i + 1, (j,))

                with sp.Fori(0, KT // 2 - 1) as i:
                    pair(i, True)
                pair(KT // 2 - 1, False)
                p2 = a["conv_pw2"][0].rearrange("(k p) n -> p k n", p=P)
                for h in range(2):
                    sp.wait_ge(part_turned, 5 + 4 * 5)
                    sp.dma_start(Wpw2[h], p2[:, 4 * h:4 * h + 4, :]).then_inc(w_in[0], 16)
                for j in range(2):
                    sp.wait_ge(val_summed[j], KT // 2)
                sp.dma_start(BROW, a["conv_pw2_b"][0].partition_broadcast(P)).then_inc(brow_in, 16)
                for L in range(2):
                    mod_rows_store(sp, L)

            @block.tensor
            def _(pe):
                with pe.Fori(0, KT // 2) as i:
                    for j in range(2):
                        pe.wait_ge(pw_in[j], i * 32 + 32)
                        pe.wait_ge(glu_done[j], i + 1)
                        for q, ((t0, lat, n, _), u, done) in enumerate(
                                ((segs[0], 0, None), (segs[0], 1, None),
                                 (segs[1], 0, gate_summed), (segs[1], 1, val_summed))):
                            for k in range(KT):
                                ins = pe.matmul(conv_bank(j, u, lat), PWB[:, j, u, k, :], HT[:, k, t0:t0 + n],
                                                start=(k == 0), stop=(k == KT - 1))
                            if done:
                                ins.then_inc(done[j], 1)
                            c = 4 * j + q - 2
                            if 1 <= c <= len(MODS):
                                L, at, m = MODS[c - 1]
                                pe.wait_ge(part_copied, i * 5 + (4 + c))
                                mod_rows_add(pe, L, i * (4 * m) + at, c - 1)
                            if 0 <= c < len(MODS):
                                pe.wait_ge(modB_in[c], i * 16 + 16)
                                mod_rows_sum(pe, 6, slot(1 + c, KT))
                pe.wait_ge(part_turned, 5 + 4 * len(MODS))
                pe.sem_inc(mod_summed[1], 1)
                for j in range(2):
                    pe.wait_ge(glu_done[j], KT // 2 + 1)
                for f in range(KT):
                    pe.wait_ge(conv_done, f + 2)
                    for c0, c1 in ((0, 512), (512, CONVW)):
                        ins = pe.matmul(MEAN[:, c0:c1], ones[:, :], V[:, f, c0:c1], start=(f == 0), stop=(f == KT - 1))
                ins.then_inc(mean_summed, 1)
                mod_rows_turn(pe, 0)
                mod_rows_turn(pe, 1)
                for f in range(KT):
                    pe.wait_ge(squared, f + 1)
                    for c0, c1 in ((0, 512), (512, CONVW)):
                        ins = pe.matmul(VAR[:, c0:c1], ones[:, :], SQ[:, f % 2, c0:c1],
                                        start=(f == 0), stop=(f == KT - 1))
                    ins.then_inc(sq_used, 1)

            @block.scalar
            def _(act):
                def copy_part(i, c):
                    act.wait_ge(part_summed, i * 5 + (5 + c))
                    act.wait_ge(part_turned, i * 5 + (1 + c))
                    nc.scalar.activation(PARTS[:, c, :], PS[:, 6, :], ACT.Copy).then_inc(part_copied, 1)

                with act.Fori(0, KT // 2) as i:
                    for j in range(2):
                        if j:
                            for c in (2, 3):
                                copy_part(i, c)
                        act.wait_ge(gate_summed[j], i + 1)
                        act.wait_ge(glu_done[j], i + 1)
                        for t0, lat, n, _ in segs:
                            ins = nc.scalar.activation(SGT[:, j, t0:t0 + n], conv_bank(j, 0, lat), ACT.Sigmoid,
                                                       bias=cols[:, bass.ds(i * 2 + (VC["conv_pw1_b"] + KT + j), 1)])
                        ins.then_inc(sig_done[j], 1)
                        for c in ((0, 1) if j == 0 else (4,)):
                            copy_part(i, c)
                for f in range(KT):
                    act.wait_ge(centred, f + 1)
                    if f >= 2:
                        act.wait_ge(sq_used, f - 1)
                    nc.scalar.activation(SQ[:, f % 2, :], V[:, f, :], ACT.Square).then_inc(squared, 1)
                act.wait_ge(var_ready, 1)
                nc.scalar.activation(STD, STD, ACT.Sqrt).then_inc(std_ready, 1)
                for f in range(KT):
                    act.wait_ge(scaled, f + 1)
                    nc.scalar.activation(V[:, f, :], V[:, f, :], ACT.Silu,
                                         scale=cols[:, VC["conv_ln_g"] + f:VC["conv_ln_g"] + f + 1],
                                         bias=cols[:, VC["conv_ln_b"] + f:VC["conv_ln_b"] + f + 1]).then_inc(z_ready, 1)

            @block.vector
            def _(dve):
                nc.vector.memset(UP[:, :, :], 0.0).then_inc(conv_step, 1)
                for one in glu_done + [conv_done]:
                    dve.sem_inc(one, 1)
                with dve.Fori(0, KT // 2) as i:
                    base = dve.snap(i * NSTEP + 1)
                    n = 0
                    for j in range(2):
                        dve.wait_ge(sig_done[j], i + 1)
                        dve.wait_ge(val_summed[j], i + 1)
                        dve.wait_ge(conv_step, base + n)
                        for (t0, lat, w, at), done in zip(segs, (conv_step, glu_done[j])):
                            nc.vector.scalar_tensor_tensor(
                                out=UP[:, j, at:at + w], in0=conv_bank(j, 1, lat),
                                scalar=cols[:, bass.ds(i * 2 + (VC["conv_pw1_b"] + j), 1)],
                                in1=SGT[:, j, t0:t0 + w], op0=ALU.add, op1=ALU.mult).then_inc(done, 1)
                        n += 1
                        dve.wait_ge(glu_done[j], i + 2)
                        dve.wait_ge(conv_done, i * 2 + (j + 1))
                        vf = V[:, bass.ds(i * 2 + j, 1), :].rearrange("p a n -> p (a n)")
                        for k in range(TAPS):
                            dve.wait_ge(conv_step, base + (n - (1 if k >= 2 else 0)))
                            w = cols[:, bass.ds(i * 2 + (DW + k * KT + j), 1)]
                            u = UP[:, j, k:k + CONVW]
                            to = vf if k % 2 == 0 else ACC2
                            if k == 0:
                                ins = nc.vector.tensor_scalar(to, u, w,
                                                              cols[:, bass.ds(i * 2 + (VC["conv_dw_b"] + j), 1)],
                                                              ALU.mult, ALU.add)
                            elif k == 1:
                                ins = nc.vector.tensor_scalar(to, u, w, None, ALU.mult)
                            else:
                                ins = nc.vector.scalar_tensor_tensor(out=to, in0=u, scalar=w, in1=to,
                                                                     op0=ALU.mult, op1=ALU.add)
                            ins.then_inc(conv_step, 1)
                            n += 1
                        dve.wait_ge(conv_step, base + n)
                        nc.vector.tensor_tensor(vf, vf, ACC2, ALU.add).then_inc(conv_done, 1)
                dve.wait_ge(mod_summed[1], 1)
                mod_columns(dve, 0, 2, NMOD)
                mod_columns(dve, 1, 0, NMOD)
                dve.wait_ge(mean_summed, 1)
                for f in range(KT):
                    nc.vector.scalar_tensor_tensor(out=V[:, f, :], in0=MEAN, scalar=-1.0 / D, in1=V[:, f, :],
                                                   op0=ALU.mult, op1=ALU.add).then_inc(centred, 1)
                for L in range(2):
                    mod_rows_copy(dve, L)
                dve.wait_ge(sq_used, KT)
                nc.vector.tensor_scalar(STD, VAR, 1.0 / D, EPS, ALU.mult, ALU.add).then_inc(var_ready, 1)
                dve.wait_ge(std_ready, 1)
                st = Steps(dve, dve_step, dve_n[0])
                st(nc.vector.reciprocal(STD, STD))
                for f in range(KT):
                    dve.wait_ge(centred, f + 1)
                    nc.vector.tensor_tensor(V[:, f, :], V[:, f, :], STD, ALU.mult).then_inc(scaled, 1)
                dve_n[0] = st.n

        H2 = RING[:, 1, 0:2 * D].rearrange("p (a n) -> p a n", a=2)
        YT = RING[:, 1, 2 * D:4 * D].rearrange("p (a n) -> p a n", a=2)

        def project_and_route(L, lhs, weights, bias, tiles, lhs_wait):
            NT = len(tiles)
            nb = MAXB[L]
            row = {0: (0, 1, 2), 1: (3, 4, 5)}

            with nc.Block() as block:
                @block.sync
                def _(sp):
                    for one in rows_out:
                        sp.wait_ge(one, 16)
                    for s in (0, 1) if NT > LT else (1,):
                        for v, w in zip((2, 4, 3), row[s]):
                            load_row(sp, L, s, v, w, rows_in[L])
                    for i in range(NT):
                        sp.wait_ge(h2_ready[L], i + 1)
                        sp.dma_start(h2d[L][i * P:(i + 1) * P, :], H2[:, i % 2, :]).then_inc(h2_out[L][i % 2], 16)
                    for b in range(2):
                        sp.wait_ge(h2_out[L][b], 16 * (NT // 2))
                    sp.wait_ge(scattered[L], 16 * 2 * NT)
                    sp.dma_start(slrow[0:nb + 1, :],
                                 slotd[L].rearrange("(b p) o -> b (p o)", p=P)).then_inc(slots_in[L], 16)

                @block.gpsimd
                def _(pool):
                    pool.wait_ge(dest_ready[L], 1)
                    for i in range(NT):
                        for c in range(2):
                            pool.indirect_dma_start(
                                out=slotd[L], out_offset=bass.IndirectOffsetOnAxis(ap=DST[:, c, i:i + 1], axis=0),
                                in_=const("tokid")[:, i:i + 1], in_offset=None).then_inc(scattered[L], 16)
                    pool.wait_ge(scattered[L], 16 * 2 * NT)

                @block.tensor
                def _(pe):
                    lhs_wait(pe)
                    for i in range(NT + 1):
                        if i < NT:
                            if i >= 2:
                                pe.wait_ge(y_used[L], i - 1)
                            for h in range(2):
                                for k in range(KT):
                                    ins = pe.matmul(PS[:, 2 * (i % 2) + h, :], lhs(i, k),
                                                    weights(k)[:, h * 512:(h + 1) * 512],
                                                    start=(k == 0), stop=(k == KT - 1))
                            ins.then_inc(y_summed[L], 1)
                        if i >= 1:
                            u = i - 1
                            pe.wait_ge(h2_ready[L], u + 1)
                            if u >= 1:
                                pe.wait_ge(h2A[L], u)
                                pe.wait_ge(h2B[L], u)
                            for k in range(KT):
                                ins = pe.transpose(PS[:, 4 + k // 4, (k % 4) * P:(k % 4 + 1) * P],
                                                   H2[:, u % 2, k * P:(k + 1) * P], ident)
                            ins.then_inc(h2_turned[L], 1)
                            pe.wait_ge(h2A[L], u + 1)
                            pe.wait_ge(h2B[L], u + 1)
                            for k in range(KT):
                                ins = pe.matmul(PS[:, 6, u * NE:(u + 1) * NE], HT[:, k, u * P:(u + 1) * P],
                                                WRT[:, k, :], start=(k == 0), stop=(k == KT - 1))
                            ins.then_inc(logits[L], 1)
                    pe.wait_ge(chosen[L], 1)
                    for i in range(NT + 1):
                        for j in range(min(i + 1, NT)):
                            ins = pe.matmul(PS[:, 7, i * NE:(i + 1) * NE], tri if j == i else ones[:, :],
                                            SEL[:, j, :], start=(j == 0), stop=(j == min(i, NT - 1)))
                    ins.then_inc(ranked[L], 1)
                    pe.wait_ge(slots_in[L], 16)
                    pe.transpose(PS[:, 0, 0:nb + 1], slrow[0:nb + 1, :], CN[0:nb + 1, 0:nb + 1]).then_inc(
                        slots_turned[L], 1)

                @block.scalar
                def _(act):
                    for i in range(NT):
                        t = tiles[i]
                        act.wait_ge(x_new[L], i + 1)
                        if i:
                            act.wait_ge(f_sq[L], i)
                        nc.scalar.activation(JUNK2, X[:, t, :], ACT.Square, accum_out=ss[:, t:t + 1]).then_inc(
                            f_sq[L], 1)
                        act.wait_ge(f_ms[L], i + 1)
                        nc.scalar.activation(rstd[:, t:t + 1], ss[:, t:t + 1], ACT.Sqrt).then_inc(f_rms[L], 1)
                        act.wait_ge(h2_turned[L], i + 1)
                        nc.scalar.activation(HT[:, 0:4, i * P:(i + 1) * P],
                                             PS[:, 4, :].rearrange("p (k n) -> p k n", k=4),
                                             ACT.Copy).then_inc(h2A[L], 1)
                    act.wait_ge(logits[L], NT)
                    nc.scalar.activation(SIG[:, 0:NT, :], PS[:, 6, 0:NT * NE].rearrange("p (t e) -> p t e", e=NE),
                                         ACT.Sigmoid).then_inc(sig_ready[L], 1)

                @block.vector
                def _(dve):
                    st = Steps(dve, dve_step, dve_n[0])
                    V_ = nc.vector
                    dve.wait_ge(rows_in[L], 16 * 3 * (2 if NT > LT else 1))
                    if bias is not None:
                        dve.wait_ge(brow_in, 16)
                    for i in range(NT):
                        t = tiles[i]
                        gr, ag, sh = row[stream(t)]
                        y = PSF[:, 1024 * (i % 2):1024 * (i % 2) + D]
                        yt = YT[:, i % 2, :]
                        h2 = H2[:, i % 2, :]
                        dve.wait_ge(y_summed[L], i + 1)
                        if bias is not None:
                            V_.tensor_tensor(yt, y, bias, ALU.add).then_inc(y_used[L], 1)
                            dve.wait_ge(y_used[L], i + 1)
                            st(V_.tensor_tensor(yt, yt, ROWS[:, gr, :], ALU.mult))
                        else:
                            V_.tensor_tensor(yt, y, ROWS[:, gr, :], ALU.mult).then_inc(y_used[L], 1)
                            dve.wait_ge(y_used[L], i + 1)
                        V_.tensor_tensor(X[:, t, :], X[:, t, :], yt, ALU.add).then_inc(x_new[L], 1)
                        dve.wait_ge(x_new[L], i + 1)
                        dve.wait_ge(f_sq[L], i + 1)
                        V_.tensor_scalar(ss[:, t:t + 1], ss[:, t:t + 1], 1.0 / D, EPS, ALU.mult,
                                         ALU.add).then_inc(f_ms[L], 1)
                        dve.wait_ge(f_rms[L], i + 1)
                        st(V_.reciprocal(rstd[:, t:t + 1], rstd[:, t:t + 1]))
                        if i >= 2:
                            dve.wait_ge(h2_out[L][i % 2], 16 * (i // 2))
                            dve.wait_ge(h2_turned[L], i - 1)
                        st(V_.scalar_tensor_tensor(out=h2, in0=X[:, t, :], scalar=rstd[:, t:t + 1],
                                                   in1=ROWS[:, ag, :], op0=ALU.mult, op1=ALU.mult))
                        V_.tensor_tensor(h2, h2, ROWS[:, sh, :], ALU.add).then_inc(h2_ready[L], 1)
                        dve.wait_ge(h2_turned[L], i + 1)
                        V_.tensor_copy(HT[:, 4:8, i * P:(i + 1) * P],
                                       PS[:, 5, :].rearrange("p (k n) -> p k n", k=4)).then_inc(h2B[L], 1)
                    dve.wait_ge(sig_ready[L], 1)
                    sig, sel, oh1, oh2 = (z[:, 0:NT, :] for z in (SIG, SEL, OH1, OH2))
                    st(V_.tensor_tensor(sel, sig, bc(rbias[:, :].unsqueeze(1), [NT, NE]), ALU.add))
                    v4 = sel.rearrange("p t (g e) -> p (t g) e", g=NG)
                    g = [G4[:, n, 0:NT * NG] for n in range(6)]
                    st(V_.tensor_tensor(g[0], v4[:, :, 0], v4[:, :, 1], ALU.max))
                    st(V_.tensor_tensor(g[1], v4[:, :, 2], v4[:, :, 3], ALU.max))
                    st(V_.tensor_tensor(g[2], v4[:, :, 0], v4[:, :, 1], ALU.add))
                    st(V_.tensor_tensor(g[3], v4[:, :, 2], v4[:, :, 3], ALU.add))
                    st(V_.tensor_tensor(g[0], g[0], g[1], ALU.add))
                    st(V_.tensor_tensor(g[2], g[2], g[3], ALU.max))
                    st(V_.tensor_tensor(g[0], g[0], g[2], ALU.max))

                    def first_largest(src, n, rev, oh, s0):
                        big, far = S6[:, s0, 0:NT], S6[:, s0 + 1, 0:NT]
                        st(V_.tensor_reduce(big, src, AX.X, ALU.max))
                        st(V_.tensor_tensor(oh, src, bc(big.unsqueeze(2), [NT, n]), ALU.is_equal))
                        st(V_.tensor_tensor(oh, oh, bc(const(rev).unsqueeze(1), [NT, n]), ALU.mult))
                        st(V_.tensor_reduce(far, oh, AX.X, ALU.max))
                        st(V_.tensor_tensor(oh, oh, bc(far.unsqueeze(2), [NT, n]), ALU.is_equal))

                    def by4(z):
                        return z.rearrange("p (t g) -> p t g", g=NG)

                    first_largest(by4(g[0]), NG, "rev4", by4(g[4]), 0)
                    st(V_.tensor_scalar(g[5], g[4], -1.0, BIG, ALU.add, ALU.mult))
                    st(V_.tensor_tensor(v4, v4, bc(g[4].unsqueeze(2), [NT * NG, NE // NG]), ALU.mult))
                    st(V_.tensor_tensor(v4, v4, bc(g[5].unsqueeze(2), [NT * NG, NE // NG]), ALU.add))
                    first_largest(sel, NE, "rev16", oh1, 0)
                    st(V_.scalar_tensor_tensor(out=sel, in0=oh1, scalar=-2 * BIG, in1=sel, op0=ALU.mult, op1=ALU.add))
                    first_largest(sel, NE, "rev16", oh2, 0)
                    tmp = TMP[:, 0:NT, :]
                    for n, oh in enumerate((oh1, oh2)):
                        st(V_.tensor_tensor(tmp, sig, oh, ALU.mult))
                        st(V_.tensor_reduce(S6[:, 2 + n, 0:NT], tmp, AX.X, ALU.add))
                    V_.tensor_tensor(sel, oh1, oh2, ALU.add).then_inc(chosen[L], 1)
                    st(V_.tensor_tensor(S6[:, 4, 0:NT], S6[:, 2, 0:NT], S6[:, 3, 0:NT], ALU.add))
                    st(V_.reciprocal(S6[:, 5, 0:NT], S6[:, 4, 0:NT]))
                    for n in range(2):
                        st(V_.tensor_tensor(GATE[:, n, 0:NT], S6[:, 2 + n, 0:NT], S6[:, 5, 0:NT], ALU.mult))
                    dve.wait_ge(ranked[L], 1)
                    cnt = E16[:, 3, :]
                    st(V_.tensor_copy(cnt, PS[:, 7, NT * NE:(NT + 1) * NE]))
                    over = TMP[:, 0:TILES, :].rearrange("p t e -> p (t e)").rearrange("p (e t) -> p e t", t=TILES)
                    st(V_.tensor_tensor(over, bc(cnt.unsqueeze(2), [NE, TILES]),
                                        bc(const("thr").unsqueeze(1), [NE, TILES]), ALU.is_gt))
                    st(V_.tensor_reduce(E16[:, 0, :], over, AX.X, ALU.add))
                    st(V_.tensor_tensor_scan(out=E16[:, 1, :], data0=ones[:, 0:NE], data1=E16[:, 0, :], initial=0.0,
                                             op0=ALU.mult, op1=ALU.add))
                    st(V_.tensor_tensor(E16[:, 2, :], E16[:, 1, :], E16[:, 0, :], ALU.subtract))
                    st(V_.tensor_scalar(E16[:, 2, :], E16[:, 2, :], float(P), None, ALU.mult))
                    st(V_.tensor_tensor(sel, PS[:, 7, 0:NT * NE].rearrange("p (t e) -> p t e", e=NE),
                                        bc(E16[:, 2, :].unsqueeze(1), [NT, NE]), ALU.add))
                    for n, oh in enumerate((oh1, oh2)):
                        st(V_.tensor_tensor(tmp, sel, oh, ALU.mult))
                        st(V_.tensor_reduce(S6[:, 2 + n, 0:NT], tmp, AX.X, ALU.add))
                        st(V_.tensor_copy(DST[:, n, 0:NT], S6[:, 2 + n, 0:NT]))
                    V_.engine_nop().then_inc(dest_ready[L], 1)
                    ends = TMP[:, 0:nb, :]
                    st(V_.tensor_tensor(ends, bc(E16[:, 1, :].unsqueeze(1), [nb, NE]),
                                        bc(const("iota")[:, 0:nb].unsqueeze(2), [nb, NE]), ALU.is_le))
                    st(V_.tensor_reduce(BLK[:, 0:nb], ends, AX.X, ALU.add))
                    st(V_.tensor_scalar(BLK[:, 0:nb], BLK[:, 0:nb], float(NE - 1), None, ALU.min))
                    st(V_.tensor_copy(INFO[:, 0:nb], BLK[:, 0:nb]))
                    n_blocks = E16[:, 1, NE - 1:NE]
                    st(V_.tensor_copy(INFO[:, MAXB[0]:MAXB[0] + 1], n_blocks))
                    st(V_.tensor_scalar(INFO[:, MAXB[0] + 1:MAXB[0] + 2], n_blocks, -1.0, None, ALU.add))
                    st(V_.tensor_scalar(INFO[:, MAXB[0] + 2:MAXB[0] + 3], n_blocks, -1.0, nb + 1.0, ALU.mult, ALU.add))
                    dve.wait_ge(slots_turned[L], 1)
                    V_.tensor_copy(IDX[:, 0:nb + 1], PS[:, 0, 0:nb + 1]).then_inc(idx_ready[L], 1)
                    dve_n[0] = st.n

        XG = ar(0, [D])
        XTT = ar(D, [KT, P])
        SIL = ar(2 * D, [FE])
        HID = ar(2 * D + FE, [FE])
        HTT = ar(2 * D + 2 * FE, [FE // P, P])
        YO = ar(3 * D + FE, [D])
        NIL = ar(5 * D, [D])
        W1S = RING[:, 0:2, :]
        W3S = RING[:, 2:4, :]
        W2S = RING[:, 4:6, :]
        PU1, PU3, PHB = PS[:, 0, :], PS[:, 1, :], PS[:, 2, :]

        def moe_blocks(L):
            nb = MAXB[L]
            least = len(range(TILES if L == 0 else LT)) * 2

            def blocks(eng):
                return eng.value_load(INFO[0:1, MAXB[0]:MAXB[0] + 1], min_val=least, max_val=nb)

            def last_block(eng):
                return eng.value_load(INFO[0:1, MAXB[0] + 1:MAXB[0] + 2], min_val=least - 1, max_val=nb - 1)

            with nc.Block() as block:
                @block.sync
                def _(sp):
                    n = blocks(sp)
                    w1 = a["moe_w1"][L].rearrange("e (k p) f -> e p k f", p=P)
                    w3 = a["moe_w3"][L].rearrange("e (k p) f -> e p k f", p=P)
                    w2 = a["moe_w2"][L].rearrange("e (k p) f -> e p k f", p=P)

                    def load(b, half, wait, freed=0):
                        e = sp.value_load(INFO[0:1, bass.ds(b, 1)], min_val=0, max_val=NE - 1)
                        if wait:
                            before = sp.compute_val(b * 16)
                        for src, dst, landed, used, k in ((w1, W1S, w1_in, w13_used, KT), (w3, W3S, w3_in, w13_used, KT),
                                                          (w2, W2S, w2_in, w2_used, FE // P)):
                            if wait:
                                sp.wait_ge(idx_ready[L], 1)
                                sp.wait_ge(landed[L], before)
                                sp.wait_ge(used[L], freed)
                            elif b == 1:
                                sp.wait_ge(landed[L], 16)
                            to = dst[:, half, :].rearrange("p a (k f) -> p (a k) f", k=k) if wait else \
                                dst[:, half, :].rearrange("p (k f) -> p k f", k=k)
                            sp.dma_start(to, src[bass.ds(e, 1)].rearrange("e p k f -> p (e k) f")).then_inc(
                                landed[L], 16)

                    load(0, 0, False)
                    load(1, 1, False)
                    with sp.Fori(1, last_block(sp)) as c:
                        load(c + 1, bass.ds((c + 1) & 1, 1), True, c)
                    sp.wait_ge(nil_set[L], 1)
                    with sp.Fori(n, nb + 1) as b:
                        sp.dma_start(yd[L][bass.ds(b * P, P), :], NIL).then_inc(nil_out[L], 16)
                    nil = sp.value_load(INFO[0:1, MAXB[0] + 2:MAXB[0] + 3], min_val=1, max_val=nb + 1 - least)
                    sp.wait_ge(nil_out[L], nil * 16)
                    load_row(sp, L, 1, 5, 1, gates_in[L])
                    sp.wait_ge(y_out[L], n * 16)
                    if L == 0:
                        load_row(sp, L, 0, 5, 0, gates_in[L])
                    else:
                        sp.dma_start(ROWS[:, 0, :], a["norm_f"].partition_broadcast(P)).then_inc(gates_in[L], 16)

                @block.gpsimd
                def _(pool):
                    n = blocks(pool)
                    src = h2d[L][:, :] if L == 0 else h2d[L][0:SEQ, :]

                    def gather():
                        pool.indirect_dma_start(out=XG, out_offset=None, in_=src,
                                                in_offset=bass.IndirectOffsetOnAxis(ap=icur[:, 0:1], axis=0)
                                                ).then_inc(xg_in[L], 16)

                    pool.tensor_copy(icur[:, :], IDX[:, 0:1]).then_inc(idx_first[L], 1)
                    pool.wait_ge(idx_first[L], 1)
                    gather()
                    with pool.Fori(1, n + 1) as b:
                        pool.wait_ge(xg_in[L], b * 16)
                        pool.wait_ge(xg_turned[L], b)
                        pool.wait_ge(idx_ready[L], 1)
                        pool.tensor_copy(icur[:, :], IDX[:, bass.ds(b, 1)]).then_inc(idx_set[L], 1)
                        pool.wait_ge(idx_ready[L], 1)
                        pool.wait_ge(idx_set[L], b)
                        gather()
                    pool.wait_ge(xg_in[L], n * 16 + 16)

                @block.tensor
                def _(pe):
                    n = blocks(pe)

                    def half(buf, h, k, c0, w, kk):
                        v = buf[:, h, :]
                        if isinstance(h, int):
                            return v.rearrange("p (k f) -> p k f", k=kk)[:, k, c0:c0 + w]
                        return v.rearrange("p a (k f) -> p (a k) f", k=kk)[:, k, c0:c0 + w]

                    def turn_x(b):
                        pe.wait_ge(xg_in[L], b * 16 + 16)
                        for k in range(KT):
                            ins = pe.transpose(PS[:, 3 + k // 4, (k % 4) * P:(k % 4 + 1) * P],
                                               XG[:, k * P:(k + 1) * P], ident)
                        ins.then_inc(xg_turned[L], 1)

                    def up(b, h, buf, bank, landed, done):
                        pe.wait_ge(landed[L], b * 16 + 16)
                        for k in range(KT):
                            ins = pe.matmul(bank, XTT[:, k, :], half(buf, h, k, 0, FE, KT),
                                            start=(k == 0), stop=(k == KT - 1))
                        ins.then_inc(done[L], 1)

                    def turn_hid(b):
                        pe.wait_ge(hid_ready[L], b + 1)
                        for k in range(FE // P):
                            ins = pe.transpose(PHB[:, k * P:(k + 1) * P], HID[:, k * P:(k + 1) * P], ident)
                        ins.then_inc(hid_turned[L], 1)

                    def down(b, h):
                        pe.wait_ge(w2_in[L], b * 16 + 16)
                        pe.wait_ge(hT_ready[L], b + 1)
                        if not (isinstance(b, int) and b == 0):
                            pe.wait_ge(ya_ready[L], b)
                            pe.wait_ge(yb_ready[L], b)
                        for c in range(2):
                            for k in range(FE // P):
                                ins = pe.matmul(PS[:, 5 + c, :], HTT[:, k, :], half(W2S, h, k, c * 512, 512, FE // P),
                                                start=(k == 0), stop=(k == FE // P - 1))
                        ins.then_inc(w2_used[L], 1)

                    turn_x(0)
                    pe.wait_ge(xTa[L], 1)
                    pe.wait_ge(xTb[L], 1)
                    up(0, 0, W1S, PU1, w1_in, up1_done)
                    up(0, 0, W3S, PU3, w3_in, w13_used)
                    turn_x(1)

                    def block_step(b, h, other):
                        pe.wait_ge(xTa[L], b + 1)
                        pe.wait_ge(xTb[L], b + 1)
                        pe.wait_ge(hid_ready[L], b)
                        up(b, h, W1S, PU1, w1_in, up1_done)
                        turn_hid(b - 1)
                        up(b, h, W3S, PU3, w3_in, w13_used)
                        turn_x(b + 1)
                        down(b - 1, other)

                    block_step(1, 1, 0)
                    with pe.Fori(2, n) as b:
                        block_step(b, bass.ds(b & 1, 1), bass.ds((b + 1) & 1, 1))
                    last = last_block(pe)
                    turn_hid(last)
                    down(last, bass.ds(last & 1, 1))

                @block.scalar
                def _(act):
                    n = blocks(act)

                    def x_half(b):
                        act.wait_ge(xg_turned[L], b + 1)
                        nc.scalar.activation(XTT[:, 0:4, :], PS[:, 3, :].rearrange("p (k n) -> p k n", k=4),
                                             ACT.Copy).then_inc(xTa[L], 1)

                    def silu(b):
                        act.wait_ge(up1_done[L], b + 1)
                        if not (isinstance(b, int) and b == 0):
                            act.wait_ge(hid_ready[L], b)
                        nc.scalar.activation(SIL, PU1, ACT.Silu).then_inc(silu_done[L], 1)

                    def hid_copy(b):
                        act.wait_ge(hid_turned[L], b + 1)
                        nc.scalar.activation(HTT[:, :, :], PHB.rearrange("p (k n) -> p k n", k=4),
                                             ACT.Copy).then_inc(hT_ready[L], 1)

                    def y_store(b, rows):
                        act.wait_ge(w2_used[L], b + 1)
                        if not (isinstance(b, int) and b == 0):
                            act.wait_ge(y_out[L], b * 16)
                        nc.scalar.activation(YO[:, 0:512], PS[:, 5, :], ACT.Copy).then_inc(ya_ready[L], 1)
                        act.wait_ge(ya_ready[L], b + 1)
                        act.wait_ge(yb_ready[L], b + 1)
                        act.dma_start(yd[L][rows, :], YO).then_inc(y_out[L], 16)

                    x_half(0)
                    silu(0)
                    act.wait_ge(w13_used[L], 1)
                    x_half(1)

                    def block_step(b, rows):
                        silu(b)
                        hid_copy(b - 1)
                        act.wait_ge(w13_used[L], b + 1)
                        x_half(b + 1)
                        y_store(b - 1, rows)

                    block_step(1, slice(0, P))
                    with act.Fori(2, n) as b:
                        block_step(b, bass.ds(b * P - P, P))
                    last = last_block(act)
                    hid_copy(last)
                    y_store(last, bass.ds(last * P, P))

                @block.vector
                def _(dve):
                    nc.vector.memset(NIL, 0.0).then_inc(nil_set[L], 1)
                    n = blocks(dve)

                    def x_half(b):
                        dve.wait_ge(xg_turned[L], b + 1)
                        nc.vector.tensor_copy(XTT[:, 4:8, :], PS[:, 4, :].rearrange("p (k n) -> p k n", k=4)).then_inc(
                            xTb[L], 1)

                    def hid(b):
                        dve.wait_ge(w13_used[L], b + 1)
                        dve.wait_ge(silu_done[L], b + 1)
                        if not (isinstance(b, int) and b == 0):
                            dve.wait_ge(hid_turned[L], b)
                        nc.vector.tensor_tensor(HID, PU3, SIL, ALU.mult).then_inc(hid_ready[L], 1)

                    def y_half(b):
                        dve.wait_ge(w2_used[L], b + 1)
                        if not (isinstance(b, int) and b == 0):
                            dve.wait_ge(y_out[L], b * 16)
                        nc.vector.tensor_copy(YO[:, 512:1024], PS[:, 6, :]).then_inc(yb_ready[L], 1)

                    x_half(0)
                    hid(0)
                    x_half(1)

                    def block_step(b):
                        hid(b)
                        x_half(b + 1)
                        y_half(b - 1)

                    block_step(1)
                    with dve.Fori(2, n) as b:
                        block_step(b)
                    y_half(last_block(dve))

        def combine_pool(pool, L, tiles):
            for i in range(len(tiles)):
                if i >= 2:
                    pool.wait_ge(x_done[L], i - 1)
                for c, done in ((0, c1_in), (1, c2_in)):
                    pool.indirect_dma_start(out=CG[:, 2 * c + i % 2, :], out_offset=None, in_=yd[L],
                                            in_offset=bass.IndirectOffsetOnAxis(ap=DST[:, c, i:i + 1], axis=0)
                                            ).then_inc(done[L][i % 2], 16)
            for b in range(2):
                pool.wait_ge(c1_in[L][b], 16 * (len(tiles) // 2))
                pool.wait_ge(c2_in[L][b], 16 * (len(tiles) // 2))

        def combine_dve(dve, L, tiles):
            st = Steps(dve, dve_step, dve_n[0])
            dve.wait_ge(gates_in[L], 32)
            for i, t in enumerate(tiles):
                c1, c2 = CG[:, i % 2, :], CG[:, 2 + i % 2, :]
                dve.wait_ge(c1_in[L][i % 2], 16 * (i // 2 + 1))
                dve.wait_ge(c2_in[L][i % 2], 16 * (i // 2 + 1))
                st(nc.vector.tensor_scalar(c1, c1, GATE[:, 0, i:i + 1], None, ALU.mult))
                st(nc.vector.scalar_tensor_tensor(out=c1, in0=c2, scalar=GATE[:, 1, i:i + 1], in1=c1,
                                                  op0=ALU.mult, op1=ALU.add))
                nc.vector.tensor_tensor(c1, c1, ROWS[:, stream(t), :], ALU.mult).then_inc(mixed[L], 1)
                dve.wait_ge(mixed[L], i + 1)
                nc.vector.tensor_tensor(X[:, t, :], X[:, t, :], c1, ALU.add).then_inc(x_done[L], 1)
            dve_n[0] = st.n

        def lhs0(i, k):
            at = i * P if i < CT else LAT0 + (i - CT) * P
            return V[:, k, at:at + P]

        def wait0(pe):
            pe.wait_ge(z_ready, KT)
            pe.wait_ge(w_in[0], 32)

        project_and_route(0, lhs0, lambda k: Wpw2[k // 4][:, k % 4, :], BROW, list(range(TILES)), wait0)
        moe_blocks(0)

        QT = RING[:, 3, :].rearrange("p (r n) -> p r n", r=8)
        KTT = ar(0, [2, TOK])
        VT = ar(2 * TOK, [TILES, NKV * DH])
        QKV = ROWS[:, 0:3, :].rearrange("p a n -> p (a n)").rearrange("p (b n) -> p b n", b=2)
        RT1 = ROWS[:, 3:5, :].rearrange("p a n -> p (a n)")[:, 0:1280]
        RT2 = ROWS[:, 4:6, :].rearrange("p a n -> p (a n)")[:, 512:512 + 1280]
        RO = RING[:, 5, 0:1280]

        with nc.Block() as block:
            @block.sync
            def _(sp):
                wq = a["attn_w_qkv"][0].rearrange("(k p) n -> p k n", p=P)
                for c in range(3):
                    sp.dma_start(slot(c, KT), wq[:, :, c * 512:(c + 1) * 512]).then_inc(wqkv_in[c], 16)

            @block.gpsimd
            def _(pool):
                combine_pool(pool, 0, list(range(TILES)))

            @block.vector
            def _(dve):
                combine_dve(dve, 0, list(range(TILES)))
                norm_dve(dve, 1)

            @block.scalar
            def _(act):
                norm_act(act, 1, lambda e, t: e.wait_ge(x_done[0], t + 1))

            @block.tensor
            def _(pe):
                norm_pe(pe, 1)

        with nc.Block() as block:
            @block.sync
            def _(sp):
                for one in again:
                    sp.sem_clear(one)
                sp.dma_start(AR[:, 3 * D:3 * D + CONSTS_W - EARLY_W], a["consts"][:, EARLY_W:CONSTS_W]).then_inc(
                    tables_in, 16)

            @block.tensor
            def _(pe):
                for c in range(3):
                    pe.wait_ge(wqkv_in[c], 16)

                def turn(u):
                    i = max(u - CT, 0)
                    pe.wait_ge(roped, u + 1)
                    if u:
                        pe.wait_ge(k_ready, u)
                        pe.wait_ge(qA_ready, max(u - CT, 0))
                        pe.wait_ge(qB_ready, max(u - CT, 0))
                    src = QKV[:, u % 2, D:D + 256] if u < CT else RO[:, D:D + 256]
                    if u >= CT:
                        for r in range(8):
                            pe.transpose(PS[:, 3 + r // 4, (r % 4) * P:(r % 4 + 1) * P],
                                         RO[:, r * P:(r + 1) * P], ident)
                    for r in range(2):
                        ins = pe.transpose(PS[:, 5, r * P:(r + 1) * P], src[:, r * P:(r + 1) * P], ident)
                    ins.then_inc(q_turned, 1)

                for t in range(TILES + 1):
                    if t < TILES:
                        if t:
                            pe.wait_ge(qkv_tok, t)
                        for c in range(3) if t >= CT else (2,):
                            for k in range(KT):
                                ins = pe.matmul(PS[:, c, :], HT[:, k, t * P:(t + 1) * P], slot(c, KT)[:, k, :],
                                                start=(k == 0), stop=(k == KT - 1))
                        ins.then_inc(qkv_summed, 1)
                    if t >= 1:
                        turn(t - 1)

            @block.scalar
            def _(act):
                for t in range(TILES):
                    act.wait_ge(qkv_summed, t + 1)
                    if t >= 2:
                        act.wait_ge(roped, t - 1)
                        act.wait_ge(v_ready, t - 1)
                        act.wait_ge(q_turned, t - 1)
                    c0 = 0 if t >= CT else 2
                    nc.scalar.activation(QKV[:, t % 2, c0 * 512:1536], PSF[:, c0 * 512:1536], ACT.Copy).then_inc(
                        qkv_tok, 1)
                    if t > CT:
                        u = t - 1
                        act.wait_ge(q_turned, u + 1)
                        j = u - CT
                        nc.scalar.activation(QT[:, 0:4, j * P:(j + 1) * P],
                                             PS[:, 3, :].rearrange("p (k n) -> p k n", k=4), ACT.Copy).then_inc(
                                                 qA_ready, 1)
                act.wait_ge(q_turned, TILES)
                j = LT - 1
                nc.scalar.activation(QT[:, 0:4, j * P:(j + 1) * P], PS[:, 3, :].rearrange("p (k n) -> p k n", k=4),
                                     ACT.Copy).then_inc(qA_ready, 1)

            @block.vector
            def _(dve):
                st = Steps(dve, dve_step, dve_n[0])
                dve.wait_ge(tables_in, 16)

                def copies(u):
                    dve.wait_ge(q_turned, u + 1)
                    if u >= CT:
                        j = u - CT
                        nc.vector.tensor_copy(QT[:, 4:8, j * P:(j + 1) * P],
                                              PS[:, 4, :].rearrange("p (k n) -> p k n", k=4)).then_inc(qB_ready, 1)
                    nc.vector.tensor_copy(KTT[:, :, u * P:(u + 1) * P],
                                          PS[:, 5, 0:2 * P].rearrange("p (k n) -> p k n", k=2)).then_inc(k_ready, 1)

                for t in range(TILES):
                    dve.wait_ge(qkv_tok, t + 1)
                    q = QKV[:, t % 2, :]
                    nc.vector.tensor_copy(VT[:, t, :], q[:, D + 256:1536]).then_inc(v_ready, 1)
                    if t < CT:
                        nc.vector.engine_nop().then_inc(roped, 1)
                        copies(t)
                        continue
                    j = t - CT
                    heads = NH + NKV
                    cos = const("cos")[:, j * DH:(j + 1) * DH]
                    sin = const("sin")[:, j * DH:(j + 1) * DH].rearrange("p (x h n) -> p x h n", x=2, h=2)
                    qh = q[:, 0:heads * DH].rearrange("p (h n) -> p h n", n=DH)
                    q4 = q[:, 0:heads * DH].rearrange("p (h x y n) -> p h x y n", x=2, y=2, n=PAIRS)
                    r4 = RT2.rearrange("p (h x y n) -> p h x y n", x=2, y=2, n=PAIRS)
                    st(nc.vector.tensor_tensor(RT1.rearrange("p (h n) -> p h n", n=DH), qh,
                                               bc(cos.unsqueeze(1), [heads, DH]), ALU.mult))
                    for y in range(2):
                        st(nc.vector.tensor_tensor(r4[:, :, :, y, :], q4[:, :, :, 1 - y, :],
                                                   bc(sin[:, :, y, :].unsqueeze(1), [heads, 2, PAIRS]), ALU.mult))
                    for p2 in range(2):
                        s0 = p2 * 512
                        to = RO[:, s0:s0 + 512].rearrange("p (r b n) -> p b r n", r=GQ, b=2)
                        i1, i2 = (z[:, s0:s0 + 512].rearrange("p (b r n) -> p b r n", b=2, r=GQ) for z in (RT1, RT2))
                        st(nc.vector.tensor_tensor(to, i1, i2, ALU.add))
                    nc.vector.tensor_tensor(RO[:, D:D + 256], RT1[:, D:D + 256], RT2[:, D:D + 256],
                                            ALU.add).then_inc(roped, 1)
                    copies(t)
                dve_n[0] = st.n

        SS = HT[:, :, :].rearrange("p k n -> p (k n)")[:, 0:4 * 640].rearrange("p (b n) -> p b n", b=4)
        PT = RING[:, 0, 0:3 * 640].rearrange("p (b n) -> p b n", b=3)
        OS = RING[:, 2, :].rearrange("p (j n) -> p j n", j=LT)
        WO = [slot(4, 4), slot(5, 4)]
        HEADS = LT * NH

        def span(j):
            return [0, 1] + [CT + m for m in range(max(j - 1, 0), min(j + 2, LT))]

        with nc.Block() as block:
            @block.sync
            def _(sp):
                wo = a["attn_w_o"][0].rearrange("(k p) n -> p k n", p=P)
                for h in range(2):
                    sp.dma_start(WO[h], wo[:, 4 * h:4 * h + 4, :]).then_inc(w_in[1], 16)

            @block.tensor
            def _(pe):
                for s in range(HEADS + 3):
                    if s < HEADS:
                        j, h = s // NH, s % NH
                        g, r = h // GQ, h % GQ
                        pr, b = g // 2, (g % 2) * DH
                        tl = span(j)
                        if s >= 2:
                            pe.wait_ge(s_masked, s - 1)
                        q = QT[b:b + DH, pr * GQ + r, j * P:(j + 1) * P]
                        to = PSF[:, 1024 * (s % 2):1024 * (s % 2) + 640]
                        pe.matmul(to[:, 0:CTX], q, KTT[b:b + DH, pr, 0:CTX], start=True, stop=True)
                        ins = pe.matmul(to[:, CTX:512], q, KTT[b:b + DH, pr, tl[2] * P:(tl[2] + 2) * P],
                                        start=True, stop=True)
                        if len(tl) == 5:
                            ins = pe.matmul(to[:, 512:640], q, KTT[b:b + DH, pr, tl[4] * P:(tl[4] + 1) * P],
                                            start=True, stop=True)
                        ins.then_inc(scored, 1)
                    u = s - 2
                    if 0 <= u < HEADS:
                        pe.wait_ge(exp_done, u + 1)
                        if u:
                            pe.wait_ge(pA_ready, u)
                            pe.wait_ge(pB_ready, u)
                        for c in range(len(span(u // NH))):
                            ins = pe.transpose(PS[:, 4 + c // 4, (c % 4) * P:(c % 4 + 1) * P],
                                               SS[:, u % 4, c * P:(c + 1) * P], ident)
                        ins.then_inc(p_turned, 1)
                    u = s - 3
                    if u >= 0:
                        j, h = u // NH, u % NH
                        tl = span(j)
                        pe.wait_ge(pA_ready, u + 1)
                        pe.wait_ge(pB_ready, u + 1)
                        if h == 0 and j:
                            pe.wait_ge(o_ready, j)
                        for c, t in enumerate(tl):
                            ins = pe.matmul(PSF[:, 3072 + h * DH:3072 + (h + 1) * DH], PT[:, u % 3, c * P:(c + 1) * P],
                                            VT[:, t, (h // GQ) * DH:(h // GQ + 1) * DH],
                                            start=(c == 0), stop=(c == len(tl) - 1))
                        ins.then_inc(av_done, 1)

            @block.vector
            def _(dve):
                st = Steps(dve, dve_step, dve_n[0])
                for s in range(HEADS + 4):
                    if s < HEADS:
                        j, h = s // NH, s % NH
                        w = len(span(j)) * P
                        dve.wait_ge(scored, s + 1)
                        if s >= 4:
                            dve.wait_ge(p_turned, s - 3)
                        mask = const("mask_first") if j == 0 else const("mask_mid")[:, 0:w]
                        nc.vector.tensor_tensor_reduce(
                            out=SS[:, s % 4, 0:w], in0=PSF[:, 1024 * (s % 2):1024 * (s % 2) + w], in1=mask,
                            scale=DH ** -0.5, scalar=sinkb[:, h:h + 1], op0=ALU.add, op1=ALU.max,
                            accum_out=mx[:, s:s + 1]).then_inc(s_masked, 1)
                        dve.wait_ge(s_masked, s + 1)
                        nc.vector.tensor_scalar(nmx[:, s:s + 1], mx[:, s:s + 1], -1.0, None, ALU.mult).then_inc(
                            neg_ready, 1)
                        if h == NH - 1:
                            nc.vector.tensor_tensor(esk[:, 0, :], sinkb[:, :], mx[:, j * NH:(j + 1) * NH],
                                                    ALU.subtract).then_inc(sinkd, 1)
                    u = s - 2
                    if 0 <= u < HEADS:
                        dve.wait_ge(p_turned, u + 1)
                        if u >= 3:
                            dve.wait_ge(av_done, u - 2)
                        nc.vector.tensor_copy(PT[:, u % 3, 0:512], PS[:, 4, :]).then_inc(pA_ready, 1)
                    u = s - 4
                    if u >= 0 and u % NH == NH - 1:
                        j = u // NH
                        dve.wait_ge(sinke, j + 1)
                        dve.wait_ge(exp_done, u + 1)
                        st(nc.vector.tensor_tensor(esk[:, 1, :], esk[:, 1, :], rsum[:, j * NH:(j + 1) * NH], ALU.add))
                        st(nc.vector.reciprocal(esk[:, 1, :], esk[:, 1, :]))
                        dve.wait_ge(av_done, u + 1)
                        nc.vector.tensor_tensor(OS[:, j, :].rearrange("p (h n) -> p h n", n=DH),
                                                PSF[:, 3072:4096].rearrange("p (h n) -> p h n", n=DH),
                                                bc(esk[:, 1, :].unsqueeze(2), [NH, DH]), ALU.mult).then_inc(o_ready, 1)
                dve_n[0] = st.n

            @block.scalar
            def _(act):
                for s in range(HEADS + 2):
                    if s < HEADS:
                        j, h = s // NH, s % NH
                        w = len(span(j)) * P
                        act.wait_ge(neg_ready, s + 1)
                        nc.scalar.activation(SS[:, s % 4, 0:w], SS[:, s % 4, 0:w], ACT.Exp, bias=nmx[:, s:s + 1],
                                             accum_out=rsum[:, s:s + 1]).then_inc(exp_done, 1)
                        if h == NH - 1:
                            act.wait_ge(sinkd, j + 1)
                            if j:
                                act.wait_ge(o_ready, j)
                            nc.scalar.activation(esk[:, 1, :], esk[:, 0, :], ACT.Exp).then_inc(sinke, 1)
                    u = s - 2
                    if 0 <= u < HEADS:
                        act.wait_ge(p_turned, u + 1)
                        if u >= 3:
                            act.wait_ge(av_done, u - 2)
                        if len(span(u // NH)) == 5:
                            nc.scalar.activation(PT[:, u % 3, 512:640], PS[:, 5, 0:P], ACT.Copy).then_inc(pB_ready, 1)
                        else:
                            act.sem_inc(pB_ready, 1)

        OT = RING[:, 3, :].rearrange("p (j k n) -> p j k n", j=LT, k=KT)
        with nc.Block() as block:
            @block.tensor
            def _(pe):
                for j in range(LT):
                    if j >= 2:
                        pe.wait_ge(oA_ready, j - 1)
                        pe.wait_ge(oB_ready, j - 1)
                    for k in range(KT):
                        ins = pe.transpose(PS[:, 2 * (j % 2) + k // 4, (k % 4) * P:(k % 4 + 1) * P],
                                           OS[:, j, k * P:(k + 1) * P], ident)
                    ins.then_inc(o_turned, 1)

            @block.scalar
            def _(act):
                for j in range(LT):
                    act.wait_ge(o_turned, j + 1)
                    nc.scalar.activation(OT[:, j, 0:4, :], PS[:, 2 * (j % 2), :].rearrange("p (k n) -> p k n", k=4),
                                         ACT.Copy).then_inc(oA_ready, 1)

            @block.vector
            def _(dve):
                for j in range(LT):
                    dve.wait_ge(o_turned, j + 1)
                    nc.vector.tensor_copy(OT[:, j, 4:8, :],
                                          PS[:, 2 * (j % 2) + 1, :].rearrange("p (k n) -> p k n", k=4)).then_inc(
                                              oB_ready, 1)

        def wait1(pe):
            pe.wait_ge(w_in[1], 32)
            pe.wait_ge(oA_ready, LT)
            pe.wait_ge(oB_ready, LT)

        lat = list(range(CT, TILES))
        project_and_route(1, lambda i, k: OT[:, i, k, :], lambda k: WO[k // 4][:, k % 4, :], None, lat, wait1)
        moe_blocks(1)

        with nc.Block() as block:
            @block.gpsimd
            def _(pool):
                combine_pool(pool, 1, lat)

            @block.vector
            def _(dve):
                combine_dve(dve, 1, lat)
                st = Steps(dve, dve_step, dve_n[0])
                for i, t in enumerate(lat):
                    dve.wait_ge(fin_ready, 2 * i + 1)
                    st(nc.vector.tensor_scalar(ss[:, t:t + 1], ss[:, t:t + 1], 1.0 / D, EPS, ALU.mult, ALU.add))
                    nc.vector.engine_nop().then_inc(centred, 1)
                    dve.wait_ge(fin_ready, 2 * i + 2)
                    st(nc.vector.reciprocal(rstd[:, t:t + 1], rstd[:, t:t + 1]))
                    st(nc.vector.scalar_tensor_tensor(out=X[:, t, :], in0=X[:, t, :], scalar=rstd[:, t:t + 1],
                                                      in1=ROWS[:, 0, :], op0=ALU.mult, op1=ALU.mult))
                    nc.vector.engine_nop().then_inc(scaled, 1)

            @block.scalar
            def _(act):
                for i, t in enumerate(lat):
                    act.wait_ge(x_done[1], i + 1)
                    if i:
                        act.wait_ge(fin_ready, 2 * i)
                    nc.scalar.activation(JUNK, X[:, t, :], ACT.Square, accum_out=ss[:, t:t + 1]).then_inc(fin_ready, 1)
                    act.wait_ge(centred, KT + i + 1)
                    nc.scalar.activation(rstd[:, t:t + 1], ss[:, t:t + 1], ACT.Sqrt).then_inc(fin_ready, 1)

            @block.sync
            def _(sp):
                o = out[0].rearrange("(t p) d -> t p d", p=P)
                for i, t in enumerate(lat):
                    sp.wait_ge(scaled, KT + i + 1)
                    sp.dma_start(o[i], X[:, t, :]).then_inc(out_sem, 16)
                sp.wait_ge(out_sem, 16 * LT)


NAMES = ["x", "c", "ctx", "c_ctx", "w_mod", "b_mod", "norm_mix", "norm_ffn", "norm_f", "conv_pw1", "conv_pw1_b",
         "conv_dw", "conv_dw_b", "conv_ln_g", "conv_ln_b", "conv_pw2", "conv_pw2_b", "attn_w_qkv", "attn_w_o",
         "attn_sink", "moe_w_router", "moe_router_bias", "moe_w1", "moe_w3", "moe_w2"]


def kernel(**inputs):
    import concourse.bacc as bacc
    from concourse.bass_utils import run_bass_kernel_spmd

    nc = bacc.Bacc("TRN2", target_bir_lowering=False, num_devices=1)
    arrays, args = {}, {}
    for name in NAMES + ["consts"]:
        v = constant_table() if name == "consts" else np.ascontiguousarray(inputs[name])
        arrays[f"in_{name}"] = v
        args[name] = nc.dram_tensor(f"in_{name}", v.shape, mybir.dt.from_np(v.dtype), kind="ExternalInput").ap()
    out = nc.dram_tensor("out_0", (1, SEQ, D), F32, kind="ExternalOutput").ap()
    build(nc, args, out)
    r = run_bass_kernel_spmd(nc, [arrays], core_ids=[0])
    return r.results[0]["out_0"]
```

```python
from contextlib import ExitStack

import numpy as np

import concourse.bass as bass
from concourse import mybir

ALU = mybir.AluOpType
ACT = mybir.ActivationFunctionType
AX = mybir.AxisListType
F32 = mybir.dt.float32
F32R = mybir.dt.float32r
I32 = mybir.dt.int32
U32 = mybir.dt.uint32

P = 128
D = 1024
KT = D // P
SEQ = 512
CTX = 256
CT = CTX // P
LT = SEQ // P
TILES = CT + LT
TOK = TILES * P
NMOD = 6
MCOLS = NMOD * KT
EPS = 1e-6
TAPS = 31
HALF = TAPS // 2
PADW = HALF + CTX + HALF + SEQ + HALF
CONVW = CTX + HALF + SEQ
LAT0 = CTX + HALF
NH = 16
DH = 64
NKV = 4
GQ = NH // NKV
NE = 16
NG = 4
FE = 512
MAXB = [TILES * 2 + NE, LT * 2 + NE]
GRID_W = 64
PAIRS = DH // 4
BIG = 1e30

CW = {}
_at = 0
for _n, _w in (("ident", P), ("tri", P), ("pick", 2), ("pick_e", NE), ("tokid", TILES), ("rev4", NG), ("rev16", NE),
               ("iota", P),
               ("thr", TILES), ("mask_mid", 5 * P), ("mask_first", 4 * P), ("cos", LT * DH), ("sin", LT * DH)):
    if _n == "mask_mid":
        EARLY_W = _at
    CW[_n] = (_at, _w)
    _at += _w
CONSTS_W = _at


def constant_table():
    t = np.zeros((P, CONSTS_W), np.float32)

    def put(name, a):
        at, w = CW[name]
        t[:, at:at + w] = a

    i = np.arange(P)
    put("ident", np.eye(P))
    put("tri", i[:, None] < i[None, :])
    put("pick", i[:, None] % (P // 4) == np.arange(2)[None, :])
    put("pick_e", i[:, None] % (P // 4) == np.arange(NE)[None, :])
    put("tokid", i[:, None] + P * np.arange(TILES)[None, :])
    put("rev4", NG - np.arange(NG)[None, :])
    put("rev16", NE - np.arange(NE)[None, :])
    put("iota", i[None, :])
    put("thr", P * np.arange(TILES)[None, :])
    low = np.where(i[None, :] >= i[:, None], 0.0, -BIG)
    up = np.where(i[None, :] <= i[:, None], 0.0, -BIG)
    nil = np.zeros((P, P))
    put("mask_mid", np.concatenate([nil, nil, low, nil, up], 1))
    put("mask_first", np.concatenate([nil, nil, nil, up], 1))
    inv = np.float32(10000.0) ** (-np.arange(PAIRS, dtype=np.float32) / np.float32(PAIRS))
    tok = np.arange(SEQ)
    ar = (tok // GRID_W).astype(np.float32)[:, None] * inv
    ac = (tok % GRID_W).astype(np.float32)[:, None] * inv
    ang = np.concatenate([ar, ar, ac, ac], -1).astype(np.float32)
    sign = np.concatenate([-np.ones(PAIRS), np.ones(PAIRS)] * 2).astype(np.float32)
    put("cos", np.cos(ang).reshape(LT, P, DH).transpose(1, 0, 2).reshape(P, -1))
    put("sin", (np.sin(ang) * sign).reshape(LT, P, DH).transpose(1, 0, 2).reshape(P, -1))
    return t


VECS = (("norm_mix", 2 * KT), ("norm_ffn", 2 * KT), ("conv_pw1_b", 2 * KT), ("conv_dw_b", KT),
        ("conv_ln_g", KT), ("conv_ln_b", KT), ("c", KT), ("c_ctx", KT))


class Steps:

    def __init__(self, eng, sem, n=0):
        self.eng, self.sem, self.n = eng, sem, n

    def __call__(self, ins):
        self.n += 1
        ins.then_inc(self.sem, 1)
        self.eng.wait_ge(self.sem, self.n)


def build(nc, a, out):
    with ExitStack() as stack:
        def sb(name, shape, dt=F32):
            return stack.enter_context(nc.sbuf_tensor(name, shape, dt))

        def sem(name):
            return stack.enter_context(nc.semaphore(name))

        def dram(name, shape, dt=F32):
            return nc.dram_tensor(name, shape, dt, kind="Internal").ap()

        X = sb("X", [P, TILES, D])
        CN = sb("CN", [P, EARLY_W])
        ones = sb("ones", [P, P])
        cols = sb("cols", [P, 96 + 88 + TAPS * KT])
        sc2 = sb("sc2", [P, KT, P // 4])
        sgc = sb("sgc", [P, 2 * KT])
        modc = sb("modc", [P, 2, 2, MCOLS])
        ss = sb("ss", [P, TILES])
        rstd = sb("rstd", [P, TILES])
        WRT = sb("WRT", [P, KT, P // 4])
        rbias = sb("rbias", [P, NE])
        E16 = sb("E16", [P, 4, NE])
        GATE = sb("GATE", [P, 2, TILES])
        DST = sb("DST", [P, 2, TILES], U32)
        IDX = sb("IDX", [P, MAXB[0] + 1], U32)
        INFO = sb("INFO", [P, MAXB[0] + 5 + NE], I32)
        N_BLOCKS, LAST_BLOCK, LAST_BUT_ONE, N_NIL, LAST_LOAD, EXPERT = range(MAXB[0], MAXB[0] + 6)
        icur = sb("icur", [P, 1], U32)
        sinkb = sb("sinkb", [P, NH])
        with ExitStack() as place:
            def shared(name, shape, dt=F32):
                return place.enter_context(nc.sbuf_tensor(name, shape, dt))

            HT = shared("HT", [P, KT, TOK])
            RING = shared("RING", [P, 6, 4096])
            ROWS = shared("ROWS", [P, 6, D])
            AR = shared("AR", [P, 8192])
        with ExitStack() as place:
            WRAW = shared("WRAW", [P, 3, 4096])
            W_HI = shared("W_HI", [P, 3, 4096], F32R)
            W_LO = shared("W_LO", [P, 3, 4096], F32R)
            XHI = shared("XHI", [P, KT, P], F32R)
            XLO = shared("XLO", [P, KT, P], F32R)
            HHI = shared("HHI", [P, FE // P, P], F32R)
            HLO = shared("HLO", [P, FE // P, P], F32R)
            XG = shared("XG", [P, D])
            SIL = shared("SIL", [P, FE])
            HID = shared("HID", [P, FE])
            YO = shared("YO", [P, D])
            NIL = shared("NIL", [P, D])
        PS = stack.enter_context(nc.psum_tensor("PS", [P, 8, 512], F32))
        vrow = ROWS[:, 0, 0:4 * P].rearrange("p (a n) -> p a n", a=4)
        PSF = PS[:, :, :].rearrange("p b n -> p (b n)")

        at = [2 * D]

        def table(a_, b_):
            at[0] += a_ * b_
            return RING[:, 0, at[0] - a_ * b_:at[0]].rearrange("p (a b) -> p a b", a=a_)

        SIG, SEL, OH1, OH2 = (table(TILES, NE) for _ in range(4))
        TMP = table(MAXB[0], NE)
        G4 = table(6, TILES * NG)
        S6 = table(8, TILES)
        BLK = table(1, MAXB[0])[:, 0, :]
        CUM = table(TILES + 1, NE)
        DEST = table(2, TILES)
        LOGT = table(2, P)

        rowsd = [dram(f"rows_of_layer{L}", [2 * NMOD, D]) for L in range(2)]
        h2d = [dram(f"moe_in{L}", [TOK, D]) for L in range(2)]
        yd = [dram(f"moe_out{L}", [(MAXB[L] + 1) * P, D]) for L in range(2)]

        def const(name, parts=P):
            at, w = CW[name]
            if at >= EARLY_W:
                return AR[:, 3 * D + at - EARLY_W:3 * D + at - EARLY_W + w]
            return CN[0:parts, at:at + w]

        ident = const("ident")
        tri = const("tri")

        BM = 0
        VC = {}
        at = 2 * MCOLS
        for n, w in VECS:
            VC[n] = at
            at += w
        DW = at

        def ar(at, shape):
            n = int(np.prod(shape))
            v = AR[:, at:at + n]
            if len(shape) == 2:
                v = v.rearrange("p (a b) -> p a b", a=shape[0])
            if len(shape) == 3:
                v = v.rearrange("p (a b c) -> p a b c", a=shape[0], b=shape[1])
            return v

        def slot(i, k):
            return RING[:, i, :].rearrange("p (k n) -> p k n", k=k)

        def bc(ap, shape):
            return ap.to_broadcast([P] + list(shape))

        def stream(t):
            return 0 if t < CT else 1

        x_in = sem("x_in")
        par_in = sem("par_in")
        dve_step = sem("dve_step")
        act_step = sem("act_step")
        ones_set = sem("ones_set")
        par_turned = sem("par_turned")
        par_cols = sem("par_cols")
        sg_done = sem("sg_done")
        sc_ready = sem("sc_ready")
        modA_in = [sem(f"modA_in{i}") for i in range(4)]
        modB_in = [sem(f"modB_in{i}") for i in range(5)]
        part_summed = sem("mod_part_summed")
        part_copied = sem("mod_part_copied")
        part_turned = sem("mod_part_turned")
        mod_summed = [sem(f"mod_summed{L}") for L in range(2)]
        mod_cols = [sem(f"mod_cols{L}") for L in range(2)]
        mod_turned = [sem(f"mod_turned{L}") for L in range(2)]
        mod_rows = [sem(f"mod_rows{L}") for L in range(2)]
        rows_out = [sem(f"rows_out{L}") for L in range(2)]
        rows_in = [sem(f"rows_in{L}") for L in range(2)]
        gates_in = [sem(f"gates_in{L}") for L in range(2)]
        sq_done = [sem("sq_done")] * 2
        ms_ready = [sem("ms_ready")] * 2
        rms_ready = [sem("rms_ready")] * 2
        xn_ready = [sem("xn_ready")] * 2
        xn_turned = [sem("xn_turned")] * 2
        hA_ready = [sem("hA_ready")] * 2
        hB_ready = [sem("hB_ready")] * 2
        before_mixer = [sq_done[0], ms_ready[0], rms_ready[0], xn_ready[0], xn_turned[0], hA_ready[0], hB_ready[0]]
        pw_in = [sem(f"pw_in{j}") for j in range(2)]
        gate_summed = [sem(f"gate_summed{j}") for j in range(2)]
        val_summed = [sem(f"val_summed{j}") for j in range(2)]
        sig_done = [sem(f"sig_done{j}") for j in range(2)]
        glu_done = [sem(f"glu_done{j}") for j in range(2)]
        conv_step = sem("conv_step")
        conv_done = sem("conv_done")
        mean_summed = sem("mean_summed")
        centred = sem("centred")
        squared = sem("squared")
        sq_used = sem("sq_used")
        var_summed = sem("var_summed")
        var_ready = sem("var_ready")
        std_ready = sem("std_ready")
        scaled = sem("scaled")
        z_ready = sem("z_ready")
        w_in = [sem(f"proj_w_in{L}") for L in range(2)]
        brow_in = sem("brow_in")
        again = []

        def both(name):
            again.append(sem(name))
            return [again[-1]] * 2

        y_summed = both("y_summed")
        y_used = both("y_used")
        x_new = both("x_new")
        f_sq = both("f_sq")
        f_ms = both("f_ms")
        f_rms = both("f_rms")
        h2_ready = both("h2_ready")
        h2_out = [[both(f"h2_out{i}")[0] for i in range(2)]] * 2
        h2_turned = both("h2_turned")
        h2A = both("h2A_ready")
        h2B = both("h2B_ready")
        logits = both("logits")
        logits_part = both("logits_part")
        logits_copied = both("logits_copied")
        sig_ready = both("sig_ready")
        chosen = both("chosen")
        ranked = both("ranked")
        info_ready = both("info_ready")
        pick_ready = both("pick_ready")
        slots_known = both("slots_known")
        idx_ready = both("idx_ready")
        w1_in = both("w1_in")
        w3_in = both("w3_in")
        w2_in = both("w2_in")
        w13_used = both("w13_used")
        w2_used = both("w2_used")
        hT_lo = both("hT_lo")
        idx_set = both("idx_set")
        idx_first = both("idx_first")
        xg_in = [sem(f"xg_in{L}") for L in range(2)]
        xg_turned = both("xg_turned")
        xTa = both("xTa_ready")
        xTb = both("xTb_ready")
        up1_done = both("up1_done")
        silu_done = both("silu_done")
        hid_ready = both("hid_ready")
        hid_turned = both("hid_turned")
        hT_ready = both("hT_ready")
        ya_ready = both("ya_ready")
        w_hi = both("w_hi")
        w_lo = both("w_lo")
        w2_hi = both("w2_hi")
        w2_lo = both("w2_lo")
        y_out = both("y_out")
        nil_set = both("nil_set")
        nil_out = both("nil_out")
        choices_in = [sem(f"choices_in{i}") for i in range(TILES)]
        c1_gated = both("choice1_gated")
        x_done = both("x_done")
        wqkv_in = [sem(f"wqkv_in{i}") for i in range(3)]
        tables_in = sem("tables_in")
        qkv_summed = sem("qkv_summed")
        qkv_tok = sem("qkv_tok")
        roped = sem("roped")
        q_turned = sem("q_turned")
        qA_ready = sem("qA_ready")
        qB_ready = sem("qB_ready")
        k_ready = sem("k_ready")
        v_ready = sem("v_ready")
        scored = sem("scored")
        s_masked = sem("s_masked")
        neg_ready = sem("neg_ready")
        exp_done = sem("exp_done")
        p_turned = sem("p_turned")
        pA_ready = sem("pA_ready")
        pB_ready = sem("pB_ready")
        av_done = sem("av_done")
        sink_exp = sem("sink_exp")
        total_inv = sem("total_inv")
        p_normed = sem("p_normed")
        oA_ready = sem("oA_ready")
        oB_ready = sem("oB_ready")
        out_sem = sem("out_sem")

        dve_n = [0]
        act_n = [0]

        def mod_sum(L, at, w=1):
            return PS[:, 7, bass.ds(at * 2 + L * 2 * MCOLS, 2 * w)]

        PARTS = ROWS[:, 0:3, :].rearrange("p a n -> p (a n)")[:, 0:2560].rearrange("p (c n) -> p c n", c=5)

        MODT = ROWS[0:2 * MCOLS, 2, 512:512 + 2 * P].rearrange("p (l n) -> p l n", l=2)

        def mod_rows_sum(pe, bank, w):
            for k in range(KT):
                g = 32 * (k % 4)
                ins = pe.matmul(PS[g:g + 32, bank, :], sc2[:, k, :], w[:, k, :], start=(k < 4), stop=(k >= 4),
                                tile_position=(0, g))
            ins.then_inc(part_summed, 1)

        def mod_rows_add(pe, L, at, c):
            for g in range(4):
                ins = pe.matmul(mod_sum(L, at + g), PARTS[:, c, g * P:(g + 1) * P], const("pick"),
                                start=True, stop=True)
            ins.then_inc(part_turned, 1)

        def mod_columns(dve, L, v0, v1):
            st = Steps(dve, dve_step, dve_n[0])
            c0, c1 = v0 * KT, v1 * KT
            pm = mod_sum(L, c0, c1 - c0).rearrange("p (m s) -> p m s", s=2)
            for s in range(2):
                st(nc.vector.tensor_tensor(modc[:, L, s, c0:c1], pm[:, :, s],
                                           cols[:, BM + L * MCOLS + c0:BM + L * MCOLS + c1], ALU.add))
            for s in range(2):
                for v, n in ((1, "norm_mix"), (4, "norm_ffn")):
                    if not v0 <= v < v1:
                        continue
                    c = modc[:, L, s, v * KT:(v + 1) * KT]
                    g = cols[:, VC[n] + L * KT:VC[n] + (L + 1) * KT]
                    st(nc.vector.scalar_tensor_tensor(out=c, in0=c, scalar=1.0, in1=g, op0=ALU.add, op1=ALU.mult))
            nc.vector.engine_nop().then_inc(mod_cols[L], 1)
            dve_n[0] = st.n

        def mod_rows_turn(pe, L):
            pe.wait_ge(mod_cols[L], 2 - L)
            pe.transpose(PS[0:2 * MCOLS, 4 + L, 0:P], modc[:, L, :, :].rearrange("p s m -> p (s m)"),
                         ident).then_inc(mod_turned[L], 1)

        def mod_rows_copy(dve, L):
            dve.wait_ge(mod_turned[L], 1)
            nc.vector.tensor_copy(MODT[:, L, :], PS[0:2 * MCOLS, 4 + L, 0:P]).then_inc(mod_rows[L], 1)

        def mod_rows_store(eng, L):
            eng.wait_ge(mod_rows[L], 1)
            eng.dma_start(rowsd[L].rearrange("v (k p) -> (v k) p", p=P), MODT[:, L, :]).then_inc(rows_out[L], 16)

        def load_row(eng, L, s, v, where, done):
            eng.dma_start(ROWS[:, where, :], rowsd[L][s * NMOD + v, :].partition_broadcast(P)).then_inc(done, 16)

        XN = ar(0, [2, D])
        JUNK = ar(2 * D, [D])
        CG = RING[:, 3:6, :].rearrange("p a (b n) -> p (a b) n", b=4)

        def turned_act(act, L, t, raw=False):
            s = stream(t)
            act.wait_ge(xn_turned[L], t + 1)
            if raw:
                nc.scalar.activation(HT[:, 0:4, t * P:(t + 1) * P],
                                     PS[:, 4 * (t % 2), :].rearrange("p (k n) -> p k n", k=4),
                                     ACT.Copy).then_inc(hA_ready[L], 1)
                return
            for k in range(KT // 2):
                ins = nc.scalar.activation(HT[:, k, t * P:(t + 1) * P], PS[:, 4 * (t % 2), k * P:(k + 1) * P],
                                           ACT.Identity, scale=modc[:, L, s, KT + k:KT + k + 1],
                                           bias=modc[:, L, s, k:k + 1])
            ins.then_inc(hA_ready[L], 1)

        def turned_dve(dve, L, u, raw=False):
            s = stream(u)
            dve.wait_ge(xn_turned[L], u + 1)
            if raw:
                nc.vector.tensor_copy(HT[:, 4:8, u * P:(u + 1) * P],
                                      PS[:, 4 * (u % 2) + 1, :].rearrange("p (k n) -> p k n", k=4)).then_inc(
                                          hB_ready[L], 1)
                return
            for k in range(KT // 2, KT):
                kk = k - KT // 2
                ins = nc.vector.tensor_scalar(HT[:, k, u * P:(u + 1) * P], PS[:, 4 * (u % 2) + 1, kk * P:(kk + 1) * P],
                                              modc[:, L, s, KT + k:KT + k + 1], modc[:, L, s, k:k + 1],
                                              ALU.mult, ALU.add)
            ins.then_inc(hB_ready[L], 1)

        def norm_act(act, L, first_wait, raw=False):
            st = Steps(act, act_step, act_n[0])
            for t in range(TILES):
                first_wait(act, t)
                if t:
                    act.wait_ge(sq_done[L], t)
                nc.scalar.activation(JUNK, X[:, t, :], ACT.Square, accum_out=ss[:, t:t + 1]).then_inc(sq_done[L], 1)
            act.wait_ge(ms_ready[L], 1)
            nc.scalar.activation(rstd[:, :], ss[:, :], ACT.Sqrt).then_inc(rms_ready[L], 1)
            for t in range(TILES):
                turned_act(act, L, t, raw)
            act_n[0] = st.n

        def norm_dve(dve, L, raw=False):
            st = Steps(dve, dve_step, dve_n[0])
            dve.wait_ge(sq_done[L], TILES)
            nc.vector.tensor_scalar(ss[:, :], ss[:, :], 1.0 / D, EPS, ALU.mult, ALU.add).then_inc(ms_ready[L], 1)
            dve.wait_ge(rms_ready[L], 1)
            st(nc.vector.reciprocal(rstd[:, :], rstd[:, :]))
            for t in range(TILES + 1):
                if t < TILES:
                    if t >= 2:
                        dve.wait_ge(xn_turned[L], t - 1)
                    nc.vector.tensor_scalar(XN[:, t % 2, :], X[:, t, :], rstd[:, t:t + 1], None,
                                            ALU.mult).then_inc(xn_ready[L], 1)
                if t >= 1:
                    turned_dve(dve, L, t - 1, raw)
            dve_n[0] = st.n

        def norm_pe(pe, L):
            for t in range(TILES):
                pe.wait_ge(xn_ready[L], t + 1)
                if t >= 2:
                    pe.wait_ge(hA_ready[L], t - 1)
                    pe.wait_ge(hB_ready[L], t - 1)
                for k in range(KT):
                    ins = pe.transpose(PS[:, 4 * (t % 2) + k // 4, (k % 4) * P:(k % 4 + 1) * P],
                                       XN[:, t % 2, k * P:(k + 1) * P], ident)
                ins.then_inc(xn_turned[L], 1)

        MOD_BANKS = (2, 3, 6, 2)
        PWB = RING[:, 0, :].rearrange("p (j u k n) -> p j u k n", j=2, u=2, k=KT)

        def load_pw(sp, i, js=range(2)):
            pw = a["conv_pw1"][0].rearrange("(k p) n -> p k n", p=P)
            for j in js:
                for u in range(2):
                    at = i * 2 * P + (j * P + (1 - u) * D)
                    sp.dma_start(PWB[:, j, u, :, :], pw[:, :, bass.ds(at, P)]).then_inc(pw_in[j], 16)

        with nc.Block() as block:
            @block.sync
            def _(sp):
                sp.dma_start(CN[:, :], a["consts"][:, 0:EARLY_W]).then_inc(par_in, 16)
                for L in range(2):
                    sp.dma_start(vrow[L * MCOLS:(L + 1) * MCOLS, 0, :],
                                 a["b_mod"][L].rearrange("(r q) -> r q", q=P)).then_inc(par_in, 16)
                at = 0
                for n, w in VECS:
                    src = a[n]
                    src = src.rearrange("(r q) -> r q", q=P) if len(src.shape) == 1 else \
                        src.rearrange("l (r q) -> (l r) q", q=P)
                    sp.dma_start(vrow[at:at + w, 1, :], src).then_inc(par_in, 16)
                    at += w
                dw = a["conv_dw"][0].rearrange("t (r q) -> (t r) q", q=P)
                for i in range(2):
                    n = TAPS * KT // 2
                    sp.dma_start(vrow[0:n, 2 + i, :], dw[i * n:(i + 1) * n, :]).then_inc(par_in, 16)
                wm = a["w_mod"][0].rearrange("(k p) n -> p k n", p=P)
                for c in range(4):
                    sp.dma_start(slot(1 + c, KT), wm[:, :, c * 512:(c + 1) * 512]).then_inc(modA_in[c], 16)
                load_pw(sp, 0)

            @block.scalar
            def _(act):
                act.dma_start(X[:, 0:CT, :], a["ctx"][0].rearrange("(t p) d -> p t d", p=P)).then_inc(x_in, 16)
                act.dma_start(X[:, CT:TILES, :], a["x"][0].rearrange("(t p) d -> p t d", p=P)).then_inc(x_in, 16)
                act.dma_start(WRT[:, :, 0:NE], a["moe_w_router"].rearrange("(k p) e -> p k e", p=P)).then_inc(par_in, 16)
                act.dma_start(rbias[:, :], a["moe_router_bias"].partition_broadcast(P)).then_inc(par_in, 16)
                act.dma_start(sinkb[:, :], a["attn_sink"][0].partition_broadcast(P)).then_inc(par_in, 16)
                act.wait_ge(par_cols, 2)
                nc.scalar.activation(sgc[:, :], cols[:, VC["c"]:VC["c"] + 2 * KT], ACT.Sigmoid).then_inc(sg_done, 1)
                norm_act(act, 0, lambda e, t: e.wait_ge(x_in, 32) if t == 0 else None, raw=True)
                for c in range(4):
                    act.wait_ge(part_summed, c + 1)
                    nc.scalar.activation(PARTS[:, c, :], PS[:, MOD_BANKS[c], :], ACT.Copy).then_inc(part_copied, 1)
                act.wait_ge(hA_ready[0], TILES)
                act.wait_ge(mod_cols[0], 1)
                for k in range(KT // 2):
                    for s, (t0, t1) in enumerate(((0, CTX), (CTX, TOK))):
                        nc.scalar.activation(HT[:, k, t0:t1], HT[:, k, t0:t1], ACT.Identity,
                                             scale=modc[:, 0, s, KT + k:KT + k + 1], bias=modc[:, 0, s, k:k + 1])

            @block.gpsimd
            def _(pool):
                pool.memset(ones[:, :], 1.0).then_inc(ones_set, 1)
                pool.memset(WRT[:, :, NE:], 0.0).then_inc(ones_set, 1)

            n_par = 1 + 2 + len(VECS) + 2 + 3

            @block.tensor
            def _(pe):
                pe.wait_ge(par_in, 16 * n_par)
                n = TAPS * KT // 2
                pe.transpose(PS[:, 0, 0:2 * MCOLS], vrow[0:2 * MCOLS, 0, :], CN[0:2 * MCOLS, 0:2 * MCOLS])
                pe.transpose(PS[:, 0, 96:184], vrow[0:88, 1, :], CN[0:88, 0:88])
                for i in range(2):
                    ins = pe.transpose(PS[:, 0, 184 + i * n:184 + (i + 1) * n], vrow[0:n, 2 + i, :], CN[0:n, 0:n])
                ins.then_inc(par_turned, 1)
                pe.wait_ge(sc_ready, 1)

                def add(c):
                    pe.wait_ge(part_copied, c + 1)
                    mod_rows_add(pe, 0, 4 * c, c)

                pe.wait_ge(modA_in[0], 16)
                mod_rows_sum(pe, MOD_BANKS[0], slot(1, KT))
                norm_pe(pe, 0)
                for c in range(1, 4):
                    pe.wait_ge(modA_in[c], 16)
                    if c == 3:
                        pe.wait_ge(part_copied, 1)
                    mod_rows_sum(pe, MOD_BANKS[c], slot(1 + c, KT))
                    add(c - 1)
                add(3)
                pe.wait_ge(part_turned, 4)
                pe.sem_inc(part_turned, 1)
                pe.sem_inc(mod_summed[0], 1)

            @block.vector
            def _(dve):
                nc.vector.memset(sc2[:, :, :], 0.0).then_inc(par_cols, 1)
                dve.wait_ge(par_turned, 1)
                nc.vector.tensor_copy(cols[:, :], PS[:, 0, 0:184 + TAPS * KT]).then_inc(par_cols, 1)
                dve.wait_ge(par_cols, 2)
                dve.wait_ge(sg_done, 1)
                for s, n in ((1, "c"), (0, "c_ctx")):
                    at = VC[n] - VC["c"]
                    ins = nc.vector.tensor_tensor(sc2[:, :, s], cols[:, VC[n]:VC[n] + KT], sgc[:, at:at + KT], ALU.mult)
                ins.then_inc(sc_ready, 1)
                norm_dve(dve, 0, raw=True)
                dve.wait_ge(mod_summed[0], 1)
                mod_columns(dve, 0, 0, 2)
                dve.wait_ge(mod_cols[0], 1)
                dve.wait_ge(hB_ready[0], TILES)
                for k in range(KT // 2, KT):
                    for s, (t0, t1) in enumerate(((0, CTX), (CTX, TOK))):
                        nc.vector.tensor_scalar(HT[:, k, t0:t1], HT[:, k, t0:t1], modc[:, 0, s, KT + k:KT + k + 1],
                                                modc[:, 0, s, k:k + 1], ALU.mult, ALU.add)

        H2 = RING[:, 1, 0:2 * D].rearrange("p (a n) -> p a n", a=2)
        YT = RING[:, 1, 2 * D:4 * D].rearrange("p (a n) -> p a n", a=2)

        LANE = RING[:, 1, 2 * D:2 * D + 2 * TILES * P].rearrange("p (q n) -> p q n", n=P)
        BLOCK = RING[:, 1, 2 * D + 2 * TILES * P:4 * D].rearrange("p (q n) -> p q n", q=16)

        def first(b):
            return isinstance(b, int) and b == 0

        def load_weights(sp, L, l, qs):
            e = sp.value_load(INFO[0:1, bass.ds(l + EXPERT, 1)], min_val=0, max_val=NE - 1)
            freed = {}
            if not first(l):
                freed = {q: sp.compute_val(l * 2 if q == 2 else l * 4 + (q * 2 - 2)) for q in qs}
            for q in qs:
                src = a[("moe_w1", "moe_w3", "moe_w2")[q]][L].rearrange("e (k p) f -> e p k f", p=P)
                if freed:
                    sp.wait_ge(idx_ready[L], 1)
                    sp.wait_ge((w2_lo if q == 2 else w_lo)[L], freed[q])
                sp.dma_start(WRAW[:, q, :].rearrange("p (k f) -> p k f", k=FE // P if q == 2 else KT),
                             src[bass.ds(e, 1)].rearrange("e p k f -> p (e k) f")).then_inc(
                                 (w1_in, w3_in, w2_in)[q][L], 16)

        def project_and_route(block, L, lhs, weights, bias, tiles, lhs_wait):
            NT = len(tiles)
            nb = MAXB[L]
            row = {0: (0, 1, 2), 1: (3, 4, 5)}

            def logit_of(u):
                return PS[:, 6 + u % 2, P + u // 2 * NE:P + (u // 2 + 1) * NE]

            @block.sync
            def _(sp):
                for one in rows_out:
                    sp.wait_ge(one, 16)
                if L == 0:
                    sp.wait_ge(scaled, KT)
                for s in (0, 1) if NT > LT else (1,):
                    for v, w in zip((2, 4, 3), row[s]):
                        load_row(sp, L, s, v, w, rows_in[L])
                for i in range(NT):
                    sp.wait_ge(h2_ready[L], i + 1)
                    sp.dma_start(h2d[L][i * P:(i + 1) * P, :], H2[:, i % 2, :]).then_inc(h2_out[L][i % 2], 16)
                for b in range(2):
                    sp.wait_ge(h2_out[L][b], 16 * (NT // 2))
                sp.wait_ge(info_ready[L], 1)
                load_weights(sp, L, 0, (0, 1))

            @block.tensor
            def _(pe):
                def add_logits(u):
                    pe.wait_ge(logits_copied[L], u + 1)
                    pe.matmul(logit_of(u), LOGT[:, u % 2, :], const("pick_e"), start=True, stop=True).then_inc(
                        logits[L], 1)

                for i in range(NT + 1):
                    if i < NT:
                        if i >= 2:
                            pe.wait_ge(y_used[L], i - 1)
                        for h in range(2):
                            for k in range(KT):
                                if i == 0 and h == 0:
                                    lhs_wait(pe, k)
                                ins = pe.matmul(PS[:, 2 * (i % 2) + h, :], lhs(i, k),
                                                weights(k)[:, h * 512:(h + 1) * 512],
                                                start=(k == 0), stop=(k == KT - 1))
                        ins.then_inc(y_summed[L], 1)
                    if i >= 1:
                        u = i - 1
                        pe.wait_ge(h2_ready[L], u + 1)
                        if u >= 1:
                            pe.wait_ge(h2A[L], u)
                            pe.wait_ge(h2B[L], u)
                        for k in range(KT):
                            ins = pe.transpose(PS[:, 4 + k // 4, (k % 4) * P:(k % 4 + 1) * P],
                                               H2[:, u % 2, k * P:(k + 1) * P], ident)
                        ins.then_inc(h2_turned[L], 1)
                        pe.wait_ge(h2A[L], u + 1)
                        pe.wait_ge(h2B[L], u + 1)
                        for k in range(KT):
                            g = 32 * (k % 4)
                            ins = pe.matmul(PS[g:g + 32, 6 + u % 2, 0:P], WRT[:, k, :], HT[:, k, u * P:(u + 1) * P],
                                            start=(k < 4), stop=(k >= 4), tile_position=(0, g))
                        ins.then_inc(logits_part[L], 1)
                        if u:
                            add_logits(u - 1)
                add_logits(NT - 1)
                pe.wait_ge(chosen[L], 1)
                pe.matmul(PS[:, 7, 0:(NT + 1) * NE], ones[:, :], CUM[:, 0:NT + 1, :].rearrange("p t e -> p (t e)"),
                          start=True, stop=False)
                pe.matmul(PS[:, 7, 0:NT * NE], tri, SEL[:, 0:NT, :].rearrange("p t e -> p (t e)"),
                          start=False, stop=True).then_inc(ranked[L], 1)
                for q in range(2 * NT):
                    pe.wait_ge(pick_ready[L], q + 1)
                    ins = pe.matmul(PS[:, 0, 0:nb + 1], LANE[:, q, :], BLOCK[:, q, 0:nb + 1],
                                    start=(q == 0), stop=(q == 2 * NT - 1))
                ins.then_inc(slots_known[L], 1)

            @block.scalar
            def _(act):
                for i in range(NT):
                    t = tiles[i]
                    act.wait_ge(x_new[L], i + 1)
                    if i:
                        act.wait_ge(f_sq[L], i)
                    nc.scalar.activation(JUNK2, X[:, t, :], ACT.Square, accum_out=ss[:, t:t + 1]).then_inc(
                        f_sq[L], 1)
                    act.wait_ge(f_ms[L], i + 1)
                    nc.scalar.activation(rstd[:, t:t + 1], ss[:, t:t + 1], ACT.Sqrt).then_inc(f_rms[L], 1)
                    act.wait_ge(h2_turned[L], i + 1)
                    nc.scalar.activation(HT[:, 0:4, i * P:(i + 1) * P],
                                         PS[:, 4, :].rearrange("p (k n) -> p k n", k=4),
                                         ACT.Copy).then_inc(h2A[L], 1)
                    act.wait_ge(logits_part[L], i + 1)
                    if i >= 2:
                        act.wait_ge(logits[L], i - 1)
                    nc.scalar.activation(LOGT[:, i % 2, :], PS[:, 6 + i % 2, 0:P], ACT.Copy).then_inc(
                        logits_copied[L], 1)
                act.wait_ge(logits[L], NT)
                for b in range(2):
                    nc.scalar.activation(SIG[:, b:NT:2, :],
                                         PS[:, 6 + b, P:P + NT // 2 * NE].rearrange("p (t e) -> p t e", e=NE),
                                         ACT.Sigmoid).then_inc(sig_ready[L], 1)

            @block.vector
            def _(dve):
                st = Steps(dve, dve_step, dve_n[0])
                V_ = nc.vector
                dve.wait_ge(rows_in[L], 16 * 3 * (2 if NT > LT else 1))
                if bias is not None:
                    dve.wait_ge(brow_in, 16)
                for i in range(NT):
                    t = tiles[i]
                    gr, ag, sh = row[stream(t)]
                    y = PSF[:, 1024 * (i % 2):1024 * (i % 2) + D]
                    yt = YT[:, i % 2, :]
                    h2 = H2[:, i % 2, :]
                    dve.wait_ge(y_summed[L], i + 1)
                    if bias is not None:
                        V_.tensor_tensor(yt, y, bias, ALU.add).then_inc(y_used[L], 1)
                        dve.wait_ge(y_used[L], i + 1)
                        st(V_.tensor_tensor(yt, yt, ROWS[:, gr, :], ALU.mult))
                    else:
                        V_.tensor_tensor(yt, y, ROWS[:, gr, :], ALU.mult).then_inc(y_used[L], 1)
                        dve.wait_ge(y_used[L], i + 1)
                    V_.tensor_tensor(X[:, t, :], X[:, t, :], yt, ALU.add).then_inc(x_new[L], 1)
                    dve.wait_ge(x_new[L], i + 1)
                    dve.wait_ge(f_sq[L], i + 1)
                    V_.tensor_scalar(ss[:, t:t + 1], ss[:, t:t + 1], 1.0 / D, EPS, ALU.mult,
                                     ALU.add).then_inc(f_ms[L], 1)
                    dve.wait_ge(f_rms[L], i + 1)
                    st(V_.reciprocal(rstd[:, t:t + 1], rstd[:, t:t + 1]))
                    if i >= 2:
                        dve.wait_ge(h2_out[L][i % 2], 16 * (i // 2))
                        dve.wait_ge(h2_turned[L], i - 1)
                    st(V_.scalar_tensor_tensor(out=h2, in0=X[:, t, :], scalar=rstd[:, t:t + 1],
                                               in1=ROWS[:, ag, :], op0=ALU.mult, op1=ALU.mult))
                    V_.tensor_tensor(h2, h2, ROWS[:, sh, :], ALU.add).then_inc(h2_ready[L], 1)
                    dve.wait_ge(h2_turned[L], i + 1)
                    V_.tensor_copy(HT[:, 4:8, i * P:(i + 1) * P],
                                   PS[:, 5, :].rearrange("p (k n) -> p k n", k=4)).then_inc(h2B[L], 1)
                dve.wait_ge(sig_ready[L], 2)
                sig, sel, oh1, oh2 = (z[:, 0:NT, :] for z in (SIG, SEL, OH1, OH2))
                st(V_.tensor_tensor(sel, sig, bc(rbias[:, :].unsqueeze(1), [NT, NE]), ALU.add))
                v4 = sel.rearrange("p t (g e) -> p (t g) e", g=NG)
                g = [G4[:, n, 0:NT * NG] for n in range(6)]
                st(V_.tensor_tensor(g[0], v4[:, :, 0], v4[:, :, 1], ALU.max))
                st(V_.tensor_tensor(g[1], v4[:, :, 2], v4[:, :, 3], ALU.max))
                st(V_.tensor_tensor(g[2], v4[:, :, 0], v4[:, :, 1], ALU.add))
                st(V_.tensor_tensor(g[3], v4[:, :, 2], v4[:, :, 3], ALU.add))
                st(V_.tensor_tensor(g[0], g[0], g[1], ALU.add))
                st(V_.tensor_tensor(g[2], g[2], g[3], ALU.max))
                st(V_.tensor_tensor(g[0], g[0], g[2], ALU.max))

                def first_largest(src, n, rev, oh, s0):
                    big, far = S6[:, s0, 0:NT], S6[:, s0 + 1, 0:NT]
                    st(V_.tensor_reduce(big, src, AX.X, ALU.max))
                    st(V_.tensor_tensor(oh, src, bc(big.unsqueeze(2), [NT, n]), ALU.is_equal))
                    st(V_.tensor_tensor(oh, oh, bc(const(rev).unsqueeze(1), [NT, n]), ALU.mult))
                    st(V_.tensor_reduce(far, oh, AX.X, ALU.max))
                    st(V_.tensor_tensor(oh, oh, bc(far.unsqueeze(2), [NT, n]), ALU.is_equal))

                def by4(z):
                    return z.rearrange("p (t g) -> p t g", g=NG)

                first_largest(by4(g[0]), NG, "rev4", by4(g[4]), 0)
                st(V_.tensor_scalar(g[5], g[4], -1.0, BIG, ALU.add, ALU.mult))
                st(V_.tensor_tensor(v4, v4, bc(g[4].unsqueeze(2), [NT * NG, NE // NG]), ALU.mult))
                st(V_.tensor_tensor(v4, v4, bc(g[5].unsqueeze(2), [NT * NG, NE // NG]), ALU.add))
                first_largest(sel, NE, "rev16", oh1, 0)
                st(V_.scalar_tensor_tensor(out=sel, in0=oh1, scalar=-2 * BIG, in1=sel, op0=ALU.mult, op1=ALU.add))
                first_largest(sel, NE, "rev16", oh2, 0)
                tmp = TMP[:, 0:NT, :]
                for n, oh in enumerate((oh1, oh2)):
                    st(V_.tensor_tensor(tmp, sig, oh, ALU.mult))
                    st(V_.tensor_reduce(S6[:, 2 + n, 0:NT], tmp, AX.X, ALU.add))
                st(V_.tensor_tensor(sel, oh1, oh2, ALU.add))
                st(V_.memset(CUM[:, 0, :], 0.0))
                for i in range(NT):
                    st(V_.tensor_tensor(CUM[:, i + 1, :], CUM[:, i, :], SEL[:, i, :], ALU.add))
                V_.engine_nop().then_inc(chosen[L], 1)
                st(V_.tensor_tensor(S6[:, 4, 0:NT], S6[:, 2, 0:NT], S6[:, 3, 0:NT], ALU.add))
                st(V_.reciprocal(S6[:, 5, 0:NT], S6[:, 4, 0:NT]))
                for n in range(2):
                    st(V_.tensor_tensor(GATE[:, n, 0:NT], S6[:, 2 + n, 0:NT], S6[:, 5, 0:NT], ALU.mult))
                dve.wait_ge(ranked[L], 1)
                cnt = E16[:, 3, :]
                st(V_.tensor_copy(cnt, PS[:, 7, NT * NE:(NT + 1) * NE]))
                over = TMP[:, 0:TILES, :].rearrange("p t e -> p (t e)").rearrange("p (e t) -> p e t", t=TILES)
                st(V_.tensor_tensor(over, bc(cnt.unsqueeze(2), [NE, TILES]),
                                    bc(const("thr").unsqueeze(1), [NE, TILES]), ALU.is_gt))
                st(V_.tensor_reduce(E16[:, 0, :], over, AX.X, ALU.add))
                st(V_.tensor_tensor_scan(out=E16[:, 1, :], data0=ones[:, 0:NE], data1=E16[:, 0, :], initial=0.0,
                                         op0=ALU.mult, op1=ALU.add))
                ends = TMP[:, 0:nb, :]
                some = E16[:, 3, :]
                st(V_.tensor_scalar(some, E16[:, 0, :], 1.0, None, ALU.min))
                st(V_.tensor_tensor(ends, bc(E16[:, 1, :].unsqueeze(1), [nb, NE]),
                                    bc(const("iota")[:, 0:nb].unsqueeze(2), [nb, NE]), ALU.is_le))
                st(V_.tensor_tensor(ends, ends, bc(some.unsqueeze(1), [nb, NE]), ALU.mult))
                st(V_.tensor_reduce(BLK[:, 0:nb], ends, AX.X, ALU.add))
                st(V_.tensor_copy(INFO[:, 0:nb], BLK[:, 0:nb]))
                n_blocks = E16[:, 1, NE - 1:NE]
                st(V_.tensor_copy(INFO[:, N_BLOCKS:N_BLOCKS + 1], n_blocks))
                st(V_.tensor_scalar(INFO[:, LAST_BLOCK:LAST_BLOCK + 1], n_blocks, -1.0, None, ALU.add))
                st(V_.tensor_scalar(INFO[:, LAST_BUT_ONE:LAST_BUT_ONE + 1], n_blocks, -2.0, None, ALU.add))
                st(V_.tensor_scalar(INFO[:, N_NIL:N_NIL + 1], n_blocks, -1.0, nb + 1.0, ALU.mult, ALU.add))
                st(V_.tensor_tensor_scan(out=E16[:, 2, :], data0=ones[:, 0:NE], data1=some, initial=0.0,
                                         op0=ALU.mult, op1=ALU.add))
                st(V_.tensor_scalar(INFO[:, LAST_LOAD:LAST_LOAD + 1], E16[:, 2, NE - 1:NE], -1.0, None, ALU.add))
                over = TMP[:, 0:NE, :]
                st(V_.tensor_tensor(over, bc(E16[:, 2, :].unsqueeze(1), [NE, NE]),
                                    bc(const("iota")[:, 0:NE].unsqueeze(2), [NE, NE]), ALU.is_le))
                st(V_.tensor_reduce(BLK[:, 0:NE], over, AX.X, ALU.add))
                st(V_.tensor_copy(INFO[:, EXPERT:EXPERT + NE], BLK[:, 0:NE]))
                V_.engine_nop().then_inc(info_ready[L], 1)
                st(V_.tensor_tensor(E16[:, 2, :], E16[:, 1, :], E16[:, 0, :], ALU.subtract))
                st(V_.tensor_scalar(E16[:, 2, :], E16[:, 2, :], float(P), None, ALU.mult))
                st(V_.tensor_tensor(sel, PS[:, 7, 0:NT * NE].rearrange("p (t e) -> p t e", e=NE),
                                    bc(E16[:, 2, :].unsqueeze(1), [NT, NE]), ALU.add))
                for n, oh in enumerate((oh1, oh2)):
                    st(V_.tensor_tensor(tmp, sel, oh, ALU.mult))
                    st(V_.tensor_reduce(S6[:, 2 + n, 0:NT], tmp, AX.X, ALU.add))
                    st(V_.tensor_copy(DST[:, n, 0:NT], S6[:, 2 + n, 0:NT]))
                dest = DEST[:, :, 0:NT].bitcast(I32)
                for to, op, x in ((S6[:, 4:6, 0:NT], ALU.bitwise_and, P - 1),
                                  (S6[:, 6:8, 0:NT], ALU.logical_shift_right, P.bit_length() - 1)):
                    st(V_.tensor_scalar(dest, DST[:, :, 0:NT].bitcast(I32), x, None, op))
                    st(V_.tensor_copy(to, dest))
                for q in range(2 * NT):
                    i, n = q // 2, q % 2
                    st(V_.tensor_scalar(LANE[:, q, :], const("iota"), S6[:, 4 + n, i:i + 1], None, ALU.is_equal))
                    V_.tensor_scalar(BLOCK[:, q, 0:nb + 1], const("iota")[:, 0:nb + 1], S6[:, 6 + n, i:i + 1],
                                     const("tokid")[:, i:i + 1], ALU.is_equal, ALU.mult).then_inc(pick_ready[L], 1)
                dve.wait_ge(slots_known[L], 1)
                V_.tensor_copy(IDX[:, 0:nb + 1], PS[:, 0, 0:nb + 1]).then_inc(idx_ready[L], 1)
                dve_n[0] = st.n

        V = ar(0, [KT, CONVW])
        UP = ar(KT * CONVW, [2, PADW])
        ACC2 = ROWS[:, 3, 0:CONVW]
        SGT = ROWS[:, 4:6, 0:TOK]
        SQ = ar(KT * CONVW, [2, CONVW])
        Wpw2 = [slot(4, 4), slot(5, 4)]
        BROW = RING[:, 0, 0:D]
        JUNK2 = RING[:, 0, D:2 * D]
        STD = ROWS[:, 3, 0:CONVW]
        MEAN = PSF[:, 0:CONVW]
        VAR = PSF[:, 1024:1024 + CONVW]
        NSTEP = 2 * (1 + TAPS)
        MODS = [(0, 2 * KT + 4 * c, 2) for c in range(2)] + [(1, 4 * c, 3) for c in range(3)]
        segs = ((0, 0, CTX, HALF), (CTX, 1, SEQ, HALF + CTX + HALF))

        def conv_bank(j, u, lat):
            return PS[:, 3 * j + u, 0:SEQ] if lat else PS[:, 3 * j + 2, u * CTX:(u + 1) * CTX]

        with nc.Block() as block:
            @block.sync
            def _(sp):
                wm = [a["w_mod"][L].rearrange("(k p) n -> p k n", p=P) for L in range(2)]
                for one in before_mixer:
                    sp.sem_clear(one)
                def pair(i, more):
                    for c, (L, at, n) in enumerate(MODS):
                        sp.wait_ge(part_turned, i * 5 + (1 + c))
                        sp.dma_start(slot(1 + c, KT),
                                     wm[L][:, :, bass.ds(i * n * 512 + at * P, 512)]).then_inc(modB_in[c], 16)
                        if more and c in (1, 4):
                            j = c // 4
                            sp.wait_ge(val_summed[j], i + 1)
                            load_pw(sp, i + 1, (j,))

                with sp.Fori(0, KT // 2 - 1) as i:
                    pair(i, True)
                pair(KT // 2 - 1, False)
                p2 = a["conv_pw2"][0].rearrange("(k p) n -> p k n", p=P)
                for h in range(2):
                    sp.wait_ge(part_turned, 5 + 4 * 5)
                    sp.dma_start(Wpw2[h], p2[:, 4 * h:4 * h + 4, :]).then_inc(w_in[0], 16)
                for j in range(2):
                    sp.wait_ge(val_summed[j], KT // 2)
                sp.dma_start(BROW, a["conv_pw2_b"][0].partition_broadcast(P)).then_inc(brow_in, 16)
                for L in range(2):
                    mod_rows_store(sp, L)

            @block.tensor
            def _(pe):
                with pe.Fori(0, KT // 2) as i:
                    for j in range(2):
                        pe.wait_ge(pw_in[j], i * 32 + 32)
                        pe.wait_ge(glu_done[j], i + 1)
                        for q, ((t0, lat, n, _), u, done) in enumerate(
                                ((segs[0], 0, None), (segs[0], 1, None),
                                 (segs[1], 0, gate_summed), (segs[1], 1, val_summed))):
                            for k in range(KT):
                                ins = pe.matmul(conv_bank(j, u, lat), PWB[:, j, u, k, :], HT[:, k, t0:t0 + n],
                                                start=(k == 0), stop=(k == KT - 1))
                            if done:
                                ins.then_inc(done[j], 1)
                            c = 4 * j + q - 2
                            if 1 <= c <= len(MODS):
                                L, at, m = MODS[c - 1]
                                pe.wait_ge(part_copied, i * 5 + (4 + c))
                                mod_rows_add(pe, L, i * (4 * m) + at, c - 1)
                            if 0 <= c < len(MODS):
                                pe.wait_ge(modB_in[c], i * 16 + 16)
                                mod_rows_sum(pe, 6, slot(1 + c, KT))
                pe.wait_ge(part_turned, 5 + 4 * len(MODS))
                pe.sem_inc(mod_summed[1], 1)
                for j in range(2):
                    pe.wait_ge(glu_done[j], KT // 2 + 1)
                for f in range(KT):
                    pe.wait_ge(conv_done, f + 2)
                    for c0, c1 in ((0, 512), (512, CONVW)):
                        ins = pe.matmul(MEAN[:, c0:c1], ones[:, :], V[:, f, c0:c1], start=(f == 0), stop=(f == KT - 1))
                ins.then_inc(mean_summed, 1)
                mod_rows_turn(pe, 0)
                mod_rows_turn(pe, 1)
                for f in range(KT):
                    pe.wait_ge(squared, f + 1)
                    for c0, c1 in ((0, 512), (512, CONVW)):
                        ins = pe.matmul(VAR[:, c0:c1], ones[:, :], SQ[:, f % 2, c0:c1],
                                        start=(f == 0), stop=(f == KT - 1))
                    ins.then_inc(sq_used, 1)

            @block.scalar
            def _(act):
                def copy_part(i, c):
                    act.wait_ge(part_summed, i * 5 + (5 + c))
                    act.wait_ge(part_turned, i * 5 + (1 + c))
                    nc.scalar.activation(PARTS[:, c, :], PS[:, 6, :], ACT.Copy).then_inc(part_copied, 1)

                with act.Fori(0, KT // 2) as i:
                    for j in range(2):
                        if j:
                            for c in (2, 3):
                                copy_part(i, c)
                        act.wait_ge(gate_summed[j], i + 1)
                        act.wait_ge(glu_done[j], i + 1)
                        for t0, lat, n, _ in segs:
                            ins = nc.scalar.activation(SGT[:, j, t0:t0 + n], conv_bank(j, 0, lat), ACT.Sigmoid,
                                                       bias=cols[:, bass.ds(i * 2 + (VC["conv_pw1_b"] + KT + j), 1)])
                        ins.then_inc(sig_done[j], 1)
                        for c in ((0, 1) if j == 0 else (4,)):
                            copy_part(i, c)
                for f in range(KT):
                    act.wait_ge(centred, f + 1)
                    if f >= 2:
                        act.wait_ge(sq_used, f - 1)
                    nc.scalar.activation(SQ[:, f % 2, :], V[:, f, :], ACT.Square).then_inc(squared, 1)
                act.wait_ge(var_ready, 1)
                nc.scalar.activation(STD, STD, ACT.Sqrt).then_inc(std_ready, 1)
                for f in range(KT):
                    act.wait_ge(scaled, f + 1)
                    nc.scalar.activation(V[:, f, :], V[:, f, :], ACT.Silu,
                                         scale=cols[:, VC["conv_ln_g"] + f:VC["conv_ln_g"] + f + 1],
                                         bias=cols[:, VC["conv_ln_b"] + f:VC["conv_ln_b"] + f + 1]).then_inc(z_ready, 1)

            @block.vector
            def _(dve):
                nc.vector.memset(UP[:, :, :], 0.0).then_inc(conv_step, 1)
                for one in glu_done + [conv_done]:
                    dve.sem_inc(one, 1)
                with dve.Fori(0, KT // 2) as i:
                    base = dve.snap(i * NSTEP + 1)
                    n = 0
                    for j in range(2):
                        dve.wait_ge(sig_done[j], i + 1)
                        dve.wait_ge(val_summed[j], i + 1)
                        dve.wait_ge(conv_step, base + n)
                        for (t0, lat, w, at), done in zip(segs, (conv_step, glu_done[j])):
                            nc.vector.scalar_tensor_tensor(
                                out=UP[:, j, at:at + w], in0=conv_bank(j, 1, lat),
                                scalar=cols[:, bass.ds(i * 2 + (VC["conv_pw1_b"] + j), 1)],
                                in1=SGT[:, j, t0:t0 + w], op0=ALU.add, op1=ALU.mult).then_inc(done, 1)
                        n += 1
                        dve.wait_ge(glu_done[j], i + 2)
                        dve.wait_ge(conv_done, i * 2 + (j + 1))
                        vf = V[:, bass.ds(i * 2 + j, 1), :].rearrange("p a n -> p (a n)")
                        for k in range(TAPS):
                            dve.wait_ge(conv_step, base + (n - (1 if k >= 2 else 0)))
                            w = cols[:, bass.ds(i * 2 + (DW + k * KT + j), 1)]
                            u = UP[:, j, k:k + CONVW]
                            to = vf if k % 2 == 0 else ACC2
                            if k == 0:
                                ins = nc.vector.tensor_scalar(to, u, w,
                                                              cols[:, bass.ds(i * 2 + (VC["conv_dw_b"] + j), 1)],
                                                              ALU.mult, ALU.add)
                            elif k == 1:
                                ins = nc.vector.tensor_scalar(to, u, w, None, ALU.mult)
                            else:
                                ins = nc.vector.scalar_tensor_tensor(out=to, in0=u, scalar=w, in1=to,
                                                                     op0=ALU.mult, op1=ALU.add)
                            ins.then_inc(conv_step, 1)
                            n += 1
                        dve.wait_ge(conv_step, base + n)
                        nc.vector.tensor_tensor(vf, vf, ACC2, ALU.add).then_inc(conv_done, 1)
                dve.wait_ge(mod_summed[1], 1)
                mod_columns(dve, 0, 2, NMOD)
                mod_columns(dve, 1, 0, NMOD)
                dve.wait_ge(mean_summed, 1)
                for f in range(KT):
                    nc.vector.scalar_tensor_tensor(out=V[:, f, :], in0=MEAN, scalar=-1.0 / D, in1=V[:, f, :],
                                                   op0=ALU.mult, op1=ALU.add).then_inc(centred, 1)
                for L in range(2):
                    mod_rows_copy(dve, L)
                dve.wait_ge(sq_used, KT)
                nc.vector.tensor_scalar(STD, VAR, 1.0 / D, EPS, ALU.mult, ALU.add).then_inc(var_ready, 1)
                dve.wait_ge(std_ready, 1)
                st = Steps(dve, dve_step, dve_n[0])
                st(nc.vector.reciprocal(STD, STD))
                for f in range(KT):
                    dve.wait_ge(centred, f + 1)
                    nc.vector.tensor_tensor(V[:, f, :], V[:, f, :], STD, ALU.mult).then_inc(scaled, 1)
                dve_n[0] = st.n

            def lhs0(i, k):
                at = i * P if i < CT else LAT0 + (i - CT) * P
                return V[:, k, at:at + P]

            def wait0(pe, k):
                if k == 0:
                    pe.wait_ge(w_in[0], 32)
                pe.wait_ge(z_ready, k + 1)

            project_and_route(block, 0, lhs0, lambda k: Wpw2[k // 4][:, k % 4, :], BROW, list(range(TILES)), wait0)

        PART = 2048
        PU1, PU3, PHB = PS[:, 0, :], PS[:, 1, :], PS[:, 2, :]

        def part(buf, q, p):
            return buf[:, q, p * PART:(p + 1) * PART]

        def split_count(q, load):
            return load * 2 + 2 if q == 2 else load * 4 + (2, 4)[q]

        def moe_blocks(L):
            nb = MAXB[L]
            least = len(range(TILES if L == 0 else LT)) * 2

            def blocks(eng):
                return eng.value_load(INFO[0:1, N_BLOCKS:N_BLOCKS + 1], min_val=least, max_val=nb)

            def last_block(eng):
                return eng.value_load(INFO[0:1, LAST_BLOCK:LAST_BLOCK + 1], min_val=least - 1, max_val=nb - 1)

            def load_of(eng, b):
                return eng.value_load(INFO[0:1, bass.ds(b, 1)], min_val=0, max_val=NE - 1)

            with nc.Block() as block:
                @block.sync
                def _(sp):
                    n = blocks(sp)
                    sp.wait_ge(xg_in[L], 16)
                    load_weights(sp, L, 0, (2,))
                    load_weights(sp, L, 1, (0, 1))
                    last_load = sp.value_load(INFO[0:1, LAST_LOAD:LAST_LOAD + 1], min_val=1, max_val=NE - 1)
                    with sp.If(last_load > 1):
                        with sp.Fori(2, last_load + 1) as l:
                            load_weights(sp, L, l, (0, 1))
                            load_weights(sp, L, l - 1, (2,))
                    load_weights(sp, L, last_load, (2,))
                    sp.wait_ge(nil_set[L], 1)
                    with sp.Fori(n, nb + 1) as b:
                        sp.dma_start(yd[L][bass.ds(b * P, P), :], NIL[:, :]).then_inc(nil_out[L], 16)
                    nil = sp.value_load(INFO[0:1, N_NIL:N_NIL + 1], min_val=1, max_val=nb + 1 - least)
                    nils, rows = sp.compute_val(nil * 16), sp.compute_val(n * 16)
                    sp.wait_ge(nil_out[L], nils)
                    sp.wait_ge(y_out[L], rows)
                    load_row(sp, L, 1, 5, 1, gates_in[L])
                    if L == 0:
                        load_row(sp, L, 0, 5, 0, gates_in[L])
                    else:
                        sp.dma_start(ROWS[:, 0, :], a["norm_f"].partition_broadcast(P)).then_inc(gates_in[L], 16)

                @block.gpsimd
                def _(pool):
                    n = blocks(pool)
                    src = h2d[L][:, :] if L == 0 else h2d[L][0:SEQ, :]

                    def gather():
                        pool.indirect_dma_start(out=XG[:, :], out_offset=None, in_=src,
                                                in_offset=bass.IndirectOffsetOnAxis(ap=icur[:, 0:1], axis=0)
                                                ).then_inc(xg_in[L], 16)

                    pool.tensor_copy(icur[:, :], IDX[:, 0:1]).then_inc(idx_first[L], 1)
                    pool.wait_ge(idx_first[L], 1)
                    gather()
                    with pool.Fori(1, n + 1) as b:
                        pool.wait_ge(xg_in[L], b * 16)
                        pool.wait_ge(xg_turned[L], b)
                        pool.wait_ge(idx_ready[L], 1)
                        pool.tensor_copy(icur[:, :], IDX[:, bass.ds(b, 1)]).then_inc(idx_set[L], 1)
                        pool.wait_ge(idx_ready[L], 1)
                        pool.wait_ge(idx_set[L], b)
                        gather()
                    pool.wait_ge(xg_in[L], n * 16 + 16)

                @block.tensor
                def _(pe):
                    n = blocks(pe)

                    def turn_x(b):
                        pe.wait_ge(xg_in[L], b * 16 + 16)
                        for k in range(KT):
                            ins = pe.transpose(PS[:, 3 + k // 4, (k % 4) * P:(k % 4 + 1) * P],
                                               XG[:, k * P:(k + 1) * P], ident)
                        ins.then_inc(xg_turned[L], 1)

                    def product(to, hi, lo, q, at, start, stop):
                        pe.matmul(to, lo, W_HI[:, q, at:at + 512], start=start, stop=False)
                        pe.matmul(to, hi, W_LO[:, q, at:at + 512], start=False, stop=False)
                        return pe.matmul(to, hi, W_HI[:, q, at:at + 512], start=False, stop=stop)

                    def up(load, q, bank, done):
                        for k in range(KT):
                            if k % 4 == 0:
                                pe.wait_ge(w_lo[L], split_count(q, load) + (k // 4 - 1))
                            ins = product(bank, XHI[:, k, :], XLO[:, k, :], q, k * FE, k == 0, k == KT - 1)
                        ins.then_inc(done[L], 1)

                    def turn_hid(b):
                        pe.wait_ge(hid_ready[L], b + 1)
                        for k in range(FE // P):
                            ins = pe.transpose(PHB[:, k * P:(k + 1) * P], HID[:, k * P:(k + 1) * P], ident)
                        ins.then_inc(hid_turned[L], 1)

                    def down(b, load):
                        pe.wait_ge(w2_lo[L], split_count(2, load))
                        pe.wait_ge(hT_lo[L], b + 1)
                        if not first(b):
                            pe.wait_ge(ya_ready[L], b)
                        for c in range(2):
                            for k in range(FE // P):
                                ins = product(PS[:, 5 + c, :], HHI[:, k, :], HLO[:, k, :], 2, k * D + c * 512,
                                              k == 0, k == FE // P - 1)
                        ins.then_inc(w2_used[L], 1)

                    turn_x(0)
                    pe.wait_ge(xTb[L], 1)
                    up(0, 0, PU1, up1_done)
                    up(0, 1, PU3, w13_used)
                    turn_x(1)

                    def block_step(b, before):
                        load = load_of(pe, b)
                        pe.wait_ge(xTb[L], b + 1)
                        pe.wait_ge(hid_ready[L], b)
                        up(load, 0, PU1, up1_done)
                        turn_hid(b - 1)
                        up(load, 1, PU3, w13_used)
                        turn_x(b + 1)
                        down(b - 1, before)

                    block_step(1, 0)
                    with pe.Fori(2, n) as b:
                        block_step(b, load_of(pe, b - 1))
                    last = last_block(pe)
                    turn_hid(last)
                    down(last, load_of(pe, last))

                @block.scalar
                def _(act):
                    n = blocks(act)

                    def split_hi(b, load, q):
                        landed = (w1_in, w3_in, w2_in)[q]
                        used = (up1_done, w13_used, w2_used)[q]
                        act.wait_ge(landed[L], load * 16 + 16)
                        if not first(b):
                            act.wait_ge(used[L], b)
                        for p in range(2):
                            nc.scalar.activation(part(W_HI, q, p), part(WRAW, q, p), ACT.Copy).then_inc(
                                (w2_hi if q == 2 else w_hi)[L], 1)

                    def split_new(b, before, load, q):
                        with act.If(before < load):
                            split_hi(b, load, q)

                    def x_hi(b):
                        act.wait_ge(xg_turned[L], b + 1)
                        if not first(b):
                            act.wait_ge(w13_used[L], b)
                        nc.scalar.activation(XHI[:, :, :],
                                             PS[:, 3:5, :].rearrange("p a (k n) -> p (a k) n", k=4),
                                             ACT.Copy).then_inc(xTa[L], 1)

                    def silu(b):
                        act.wait_ge(up1_done[L], b + 1)
                        if not first(b):
                            act.wait_ge(hid_ready[L], b)
                        nc.scalar.activation(SIL[:, :], PU1, ACT.Silu).then_inc(silu_done[L], 1)

                    def hid_hi(b):
                        act.wait_ge(hid_turned[L], b + 1)
                        nc.scalar.activation(HHI[:, :, :], PHB.rearrange("p (k n) -> p k n", k=4),
                                             ACT.Copy).then_inc(hT_ready[L], 1)

                    def y_store(b, rows):
                        act.wait_ge(w2_used[L], b + 1)
                        if not first(b):
                            act.wait_ge(y_out[L], b * 16)
                        nc.scalar.activation(YO[:, :].rearrange("p (a n) -> p a n", a=2), PS[:, 5:7, :],
                                             ACT.Copy).then_inc(ya_ready[L], 1)
                        act.wait_ge(ya_ready[L], b + 1)
                        act.dma_start(yd[L][rows, :], YO[:, :]).then_inc(y_out[L], 16)

                    split_hi(0, 0, 0)
                    x_hi(0)
                    split_hi(0, 0, 1)
                    silu(0)

                    def block_step(b, rows):
                        before, load = load_of(act, b - 1), load_of(act, b)
                        split_new(b, before, load, 0)
                        x_hi(b)
                        split_new(b, before, load, 1)
                        if rows is not None:
                            y_store(b - 2, rows)
                            split_new(b - 1, load_of(act, b - 2), before, 2)
                        else:
                            split_hi(0, 0, 2)
                        silu(b)
                        hid_hi(b - 1)

                    block_step(1, None)
                    block_step(2, slice(0, P))
                    with act.Fori(3, n) as b:
                        block_step(b, bass.ds(b * P - 2 * P, P))
                    last = last_block(act)
                    y_store(act.value_load(INFO[0:1, LAST_BUT_ONE:LAST_BUT_ONE + 1], min_val=least - 2, max_val=nb - 2),
                            bass.ds(last * P - P, P))
                    split_new(last, load_of(act, last - 1), load_of(act, last), 2)
                    hid_hi(last)
                    y_store(last, bass.ds(last * P, P))

                @block.vector
                def _(dve):
                    nc.vector.memset(NIL[:, :], 0.0).then_inc(nil_set[L], 1)
                    n = blocks(dve)

                    def split_lo(load, q):
                        hi, lo = (w2_hi, w2_lo) if q == 2 else (w_hi, w_lo)
                        for p in range(2):
                            dve.wait_ge(hi[L], split_count(q, load) + (p - 1))
                            nc.vector.tensor_tensor(part(W_LO, q, p), part(WRAW, q, p), part(W_HI, q, p).bitcast(F32),
                                                    ALU.subtract).then_inc(lo[L], 1)

                    def split_new(before, load, q):
                        with dve.If(before < load):
                            split_lo(load, q)

                    def x_lo(b):
                        dve.wait_ge(xTa[L], b + 1)
                        nc.vector.tensor_tensor(XLO[:, :, :], PS[:, 3:5, :].rearrange("p a (k n) -> p (a k) n", k=4),
                                                XHI[:, :, :].bitcast(F32), ALU.subtract).then_inc(xTb[L], 1)

                    def hid(b):
                        dve.wait_ge(w13_used[L], b + 1)
                        dve.wait_ge(silu_done[L], b + 1)
                        if not first(b):
                            dve.wait_ge(hid_turned[L], b)
                        nc.vector.tensor_tensor(HID[:, :], PU3, SIL[:, :], ALU.mult).then_inc(hid_ready[L], 1)

                    def hid_lo(b):
                        dve.wait_ge(hT_ready[L], b + 1)
                        nc.vector.tensor_tensor(HLO[:, :, :], PHB.rearrange("p (k n) -> p k n", k=4),
                                                HHI[:, :, :].bitcast(F32),
                                                ALU.subtract).then_inc(hT_lo[L], 1)

                    split_lo(0, 0)
                    x_lo(0)
                    split_lo(0, 1)

                    def block_step(b):
                        before, load = load_of(dve, b - 1), load_of(dve, b)
                        split_new(before, load, 0)
                        hid(b - 1)
                        x_lo(b)
                        split_new(before, load, 1)
                        if isinstance(b, int) and b == 1:
                            split_lo(0, 2)
                        else:
                            split_new(load_of(dve, b - 2), before, 2)
                        hid_lo(b - 1)

                    block_step(1)
                    with dve.Fori(2, n) as b:
                        block_step(b)
                    last = last_block(dve)
                    hid(last)
                    split_new(load_of(dve, last - 1), load_of(dve, last), 2)
                    hid_lo(last)

        combine_norm = [(sq_done[1], ms_ready[1], rms_ready[1]), (f_sq[1], f_ms[1], f_rms[1])]

        def combine_pool(pool, L, tiles):
            for i in range(len(tiles)):
                for c in range(2):
                    pool.indirect_dma_start(out=CG[:, 2 * i + c, :], out_offset=None, in_=yd[L],
                                            in_offset=bass.IndirectOffsetOnAxis(ap=DST[:, c, i:i + 1], axis=0)
                                            ).then_inc(choices_in[i], 16)
            for i in range(len(tiles)):
                pool.wait_ge(choices_in[i], 32 * (L + 1))

        def combine_act(act, L, tiles, base, after):
            sq, _, rms = combine_norm[L]
            for i in range(len(tiles) + 2):
                if i < len(tiles):
                    act.wait_ge(choices_in[i], 32 * (L + 1))
                    nc.scalar.activation(CG[:, 2 * i, :], CG[:, 2 * i, :], ACT.Copy,
                                         scale=GATE[:, 0, i:i + 1]).then_inc(c1_gated[L], 1)
                if 1 <= i <= len(tiles):
                    t = tiles[i - 1]
                    act.wait_ge(x_done[L], i)
                    if i >= 2:
                        act.wait_ge(sq, base + i - 1)
                    nc.scalar.activation(JUNK, X[:, t, :], ACT.Square, accum_out=ss[:, t:t + 1]).then_inc(sq, 1)
                    act.wait_ge(combine_norm[L][1], base + i)
                    nc.scalar.activation(rstd[:, t:t + 1], ss[:, t:t + 1], ACT.Sqrt).then_inc(rms, 1)
                if i >= 2:
                    after(i - 2)

        def combine_dve(dve, L, tiles, base, after, last):
            sq, ms, rms = combine_norm[L]
            st = Steps(dve, dve_step, dve_n[0])
            dve.wait_ge(gates_in[L], 32)
            for i in range(len(tiles) + 2):
                c1, c2 = (CG[:, 2 * i + c, :] if i < len(tiles) else None for c in range(2))
                if i < len(tiles):
                    dve.wait_ge(choices_in[i], 32 * (L + 1))
                    dve.wait_ge(c1_gated[L], i + 1)
                    st(nc.vector.scalar_tensor_tensor(out=c1, in0=c2, scalar=GATE[:, 1, i:i + 1], in1=c1,
                                                      op0=ALU.mult, op1=ALU.add))
                if 1 <= i <= len(tiles):
                    t = tiles[i - 1]
                    dve.wait_ge(sq, base + i)
                    nc.vector.tensor_scalar(ss[:, t:t + 1], ss[:, t:t + 1], 1.0 / D, EPS, ALU.mult,
                                            ALU.add).then_inc(ms, 1)
                if i < len(tiles):
                    st(nc.vector.tensor_tensor(c1, c1, ROWS[:, stream(tiles[i]), :], ALU.mult))
                    nc.vector.tensor_tensor(X[:, tiles[i], :], X[:, tiles[i], :], c1, ALU.add).then_inc(x_done[L], 1)
                if 1 <= i <= len(tiles):
                    t = tiles[i - 1]
                    dve.wait_ge(rms, base + i)
                    st(nc.vector.reciprocal(rstd[:, t:t + 1], rstd[:, t:t + 1]))
                    after(i - 1)
                if i >= 2:
                    last(i - 2)
            dve_n[0] = st.n

        moe_blocks(0)

        QT = RING[:, 3, :].rearrange("p (r n) -> p r n", r=8)
        KTT = ar(0, [2, TOK])
        VT = ar(2 * TOK, [TILES, NKV * DH])
        QKV = ROWS[:, 0:3, :].rearrange("p a n -> p (a n)").rearrange("p (b n) -> p b n", b=2)
        RT1 = ROWS[:, 3:5, :].rearrange("p a n -> p (a n)")[:, 0:1280]
        RT2 = ROWS[:, 4:6, :].rearrange("p a n -> p (a n)")[:, 512:512 + 1280]
        RO = RING[:, 5, 0:1280]

        with nc.Block() as block:
            @block.sync
            def _(sp):
                wq = a["attn_w_qkv"][0].rearrange("(k p) n -> p k n", p=P)
                sp.wait_ge(choices_in[3], 32)
                for c in range(3):
                    sp.dma_start(slot(c, KT), wq[:, :, c * 512:(c + 1) * 512]).then_inc(wqkv_in[c], 16)

            @block.gpsimd
            def _(pool):
                combine_pool(pool, 0, list(range(TILES)))

            @block.vector
            def _(dve):
                def normed(u):
                    if u >= 2:
                        dve.wait_ge(xn_turned[1], u - 1)
                    nc.vector.tensor_scalar(XN[:, u % 2, :], X[:, u, :], rstd[:, u:u + 1], None,
                                            ALU.mult).then_inc(xn_ready[1], 1)

                combine_dve(dve, 0, list(range(TILES)), 0, normed, lambda u: turned_dve(dve, 1, u))

            @block.scalar
            def _(act):
                combine_act(act, 0, list(range(TILES)), 0, lambda u: turned_act(act, 1, u))

            @block.tensor
            def _(pe):
                norm_pe(pe, 1)

        with nc.Block() as block:
            @block.sync
            def _(sp):
                for one in again:
                    sp.sem_clear(one)
                sp.dma_start(AR[:, 3 * D:3 * D + CONSTS_W - EARLY_W], a["consts"][:, EARLY_W:CONSTS_W]).then_inc(
                    tables_in, 16)

            @block.tensor
            def _(pe):
                for c in range(3):
                    pe.wait_ge(wqkv_in[c], 16)

                def turn(u):
                    i = max(u - CT, 0)
                    pe.wait_ge(roped, u + 1)
                    if u:
                        pe.wait_ge(k_ready, u)
                        pe.wait_ge(qA_ready, max(u - CT, 0))
                        pe.wait_ge(qB_ready, max(u - CT, 0))
                    src = QKV[:, u % 2, D:D + 256] if u < CT else RO[:, D:D + 256]
                    if u >= CT:
                        for r in range(8):
                            pe.transpose(PS[:, 3 + r // 4, (r % 4) * P:(r % 4 + 1) * P],
                                         RO[:, r * P:(r + 1) * P], ident)
                    for r in range(2):
                        ins = pe.transpose(PS[:, 5, r * P:(r + 1) * P], src[:, r * P:(r + 1) * P], ident)
                    ins.then_inc(q_turned, 1)

                for t in range(TILES + 1):
                    if t < TILES:
                        if t:
                            pe.wait_ge(qkv_tok, t)
                        for c in range(3) if t >= CT else (2,):
                            for k in range(KT):
                                ins = pe.matmul(PS[:, c, :], HT[:, k, t * P:(t + 1) * P], slot(c, KT)[:, k, :],
                                                start=(k == 0), stop=(k == KT - 1))
                        ins.then_inc(qkv_summed, 1)
                    if t >= 1:
                        turn(t - 1)

            @block.scalar
            def _(act):
                for t in range(TILES):
                    act.wait_ge(qkv_summed, t + 1)
                    if t >= 2:
                        act.wait_ge(roped, t - 1)
                        act.wait_ge(v_ready, t - 1)
                        act.wait_ge(q_turned, t - 1)
                    c0 = 0 if t >= CT else 2
                    nc.scalar.activation(QKV[:, t % 2, c0 * 512:1536], PSF[:, c0 * 512:1536], ACT.Copy).then_inc(
                        qkv_tok, 1)
                    if t > CT:
                        u = t - 1
                        act.wait_ge(q_turned, u + 1)
                        j = u - CT
                        nc.scalar.activation(QT[:, 0:4, j * P:(j + 1) * P],
                                             PS[:, 3, :].rearrange("p (k n) -> p k n", k=4), ACT.Copy).then_inc(
                                                 qA_ready, 1)
                act.wait_ge(q_turned, TILES)
                j = LT - 1
                nc.scalar.activation(QT[:, 0:4, j * P:(j + 1) * P], PS[:, 3, :].rearrange("p (k n) -> p k n", k=4),
                                     ACT.Copy).then_inc(qA_ready, 1)

            @block.vector
            def _(dve):
                st = Steps(dve, dve_step, dve_n[0])
                dve.wait_ge(tables_in, 16)

                def copies(u):
                    dve.wait_ge(q_turned, u + 1)
                    if u >= CT:
                        j = u - CT
                        nc.vector.tensor_copy(QT[:, 4:8, j * P:(j + 1) * P],
                                              PS[:, 4, :].rearrange("p (k n) -> p k n", k=4)).then_inc(qB_ready, 1)
                    nc.vector.tensor_copy(KTT[:, :, u * P:(u + 1) * P],
                                          PS[:, 5, 0:2 * P].rearrange("p (k n) -> p k n", k=2)).then_inc(k_ready, 1)

                for t in range(TILES):
                    dve.wait_ge(qkv_tok, t + 1)
                    q = QKV[:, t % 2, :]
                    nc.vector.tensor_copy(VT[:, t, :], q[:, D + 256:1536]).then_inc(v_ready, 1)
                    if t < CT:
                        nc.vector.engine_nop().then_inc(roped, 1)
                        copies(t)
                        continue
                    j = t - CT
                    heads = NH + NKV
                    cos = const("cos")[:, j * DH:(j + 1) * DH]
                    sin = const("sin")[:, j * DH:(j + 1) * DH].rearrange("p (x h n) -> p x h n", x=2, h=2)
                    qh = q[:, 0:heads * DH].rearrange("p (h n) -> p h n", n=DH)
                    q4 = q[:, 0:heads * DH].rearrange("p (h x y n) -> p h x y n", x=2, y=2, n=PAIRS)
                    r4 = RT2.rearrange("p (h x y n) -> p h x y n", x=2, y=2, n=PAIRS)
                    st(nc.vector.tensor_tensor(RT1.rearrange("p (h n) -> p h n", n=DH), qh,
                                               bc(cos.unsqueeze(1), [heads, DH]), ALU.mult))
                    for y in range(2):
                        st(nc.vector.tensor_tensor(r4[:, :, :, y, :], q4[:, :, :, 1 - y, :],
                                                   bc(sin[:, :, y, :].unsqueeze(1), [heads, 2, PAIRS]), ALU.mult))
                    for p2 in range(2):
                        s0 = p2 * 512
                        to = RO[:, s0:s0 + 512].rearrange("p (r b n) -> p b r n", r=GQ, b=2)
                        i1, i2 = (z[:, s0:s0 + 512].rearrange("p (b r n) -> p b r n", b=2, r=GQ) for z in (RT1, RT2))
                        st(nc.vector.tensor_tensor(to, i1, i2, ALU.add))
                    nc.vector.tensor_tensor(RO[:, D:D + 256], RT1[:, D:D + 256], RT2[:, D:D + 256],
                                            ALU.add).then_inc(roped, 1)
                    copies(t)
                dve_n[0] = st.n

        SS = HT[:, :, :].rearrange("p k n -> p (k n)")[:, 0:5 * 640].rearrange("p (b n) -> p b n", b=5)
        PT = RING[:, 0, 0:3 * 640].rearrange("p (b n) -> p b n", b=3)
        OT = RING[:, 2, :].rearrange("p (j k n) -> p j k n", j=LT, k=KT)
        WO = [slot(4, 4), slot(5, 4)]
        HEADS = LT * NH
        mx, nmx, rsum, esk = (AR[:, 5 * D + i * HEADS:5 * D + (i + 1) * HEADS] for i in range(4))

        def span(j):
            return [0, 1] + [CT + m for m in range(max(j - 1, 0), min(j + 2, LT))]

        with nc.Block() as block:
            @block.sync
            def _(sp):
                wo = a["attn_w_o"][0].rearrange("(k p) n -> p k n", p=P)
                for h in range(2):
                    sp.dma_start(WO[h], wo[:, 4 * h:4 * h + 4, :]).then_inc(w_in[1], 16)

            @block.tensor
            def _(pe):
                for s in range(HEADS + 4):
                    if s < HEADS:
                        j, h = s // NH, s % NH
                        g, r = h // GQ, h % GQ
                        pr, b = g // 2, (g % 2) * DH
                        tl = span(j)
                        if s >= 2:
                            pe.wait_ge(s_masked, s - 1)
                        q = QT[b:b + DH, pr * GQ + r, j * P:(j + 1) * P]
                        to = PSF[:, 1024 * (s % 2):1024 * (s % 2) + 640]
                        pe.matmul(to[:, 0:CTX], q, KTT[b:b + DH, pr, 0:CTX], start=True, stop=True)
                        ins = pe.matmul(to[:, CTX:512], q, KTT[b:b + DH, pr, tl[2] * P:(tl[2] + 2) * P],
                                        start=True, stop=True)
                        if len(tl) == 5:
                            ins = pe.matmul(to[:, 512:640], q, KTT[b:b + DH, pr, tl[4] * P:(tl[4] + 1) * P],
                                            start=True, stop=True)
                        ins.then_inc(scored, 1)
                    u = s - 3
                    if 0 <= u < HEADS:
                        pe.wait_ge(p_normed, u + 1)
                        if u:
                            pe.wait_ge(pA_ready, u)
                            pe.wait_ge(pB_ready, u)
                        for c in range(len(span(u // NH))):
                            ins = pe.transpose(PS[:, 4 + c // 4, (c % 4) * P:(c % 4 + 1) * P],
                                               SS[:, u % 5, c * P:(c + 1) * P], ident)
                        ins.then_inc(p_turned, 1)
                    u = s - 4
                    if u >= 0:
                        j, h = u // NH, u % NH
                        tl = span(j)
                        b, k = (h % 2) * DH, h // 2
                        pe.wait_ge(pA_ready, u + 1)
                        pe.wait_ge(pB_ready, u + 1)
                        if h == 0 and j:
                            pe.wait_ge(oA_ready, j)
                            pe.wait_ge(oB_ready, j)
                        for c, t in enumerate(tl):
                            ins = pe.matmul(PS[b:b + DH, 6 + k // 4, (k % 4) * P:(k % 4 + 1) * P],
                                            VT[:, t, (h // GQ) * DH:(h // GQ + 1) * DH], PT[:, u % 3, c * P:(c + 1) * P],
                                            start=(c == 0), stop=(c == len(tl) - 1), tile_position=(0, b))
                        ins.then_inc(av_done, 1)

            @block.vector
            def _(dve):
                st = Steps(dve, dve_step, dve_n[0])
                for s in range(HEADS + 4):
                    if s < HEADS:
                        j, h = s // NH, s % NH
                        w = len(span(j)) * P
                        dve.wait_ge(scored, s + 1)
                        if s >= 5:
                            dve.wait_ge(p_turned, s - 4)
                        mask = const("mask_first") if j == 0 else const("mask_mid")[:, 0:w]
                        nc.vector.tensor_tensor_reduce(
                            out=SS[:, s % 5, 0:w], in0=PSF[:, 1024 * (s % 2):1024 * (s % 2) + w], in1=mask,
                            scale=DH ** -0.5, scalar=sinkb[:, h:h + 1], op0=ALU.add, op1=ALU.max,
                            accum_out=mx[:, s:s + 1]).then_inc(s_masked, 1)
                        dve.wait_ge(s_masked, s + 1)
                        nc.vector.tensor_scalar(nmx[:, s:s + 1], mx[:, s:s + 1], -1.0, None, ALU.mult).then_inc(
                            neg_ready, 1)
                    u = s - 1
                    if 0 <= u < HEADS:
                        dve.wait_ge(exp_done, u + 1)
                        dve.wait_ge(sink_exp, u + 1)
                        st(nc.vector.tensor_tensor(esk[:, u:u + 1], esk[:, u:u + 1], rsum[:, u:u + 1], ALU.add))
                        nc.vector.reciprocal(esk[:, u:u + 1], esk[:, u:u + 1]).then_inc(total_inv, 1)
                    u = s - 3
                    if 0 <= u < HEADS:
                        dve.wait_ge(p_turned, u + 1)
                        if u >= 3:
                            dve.wait_ge(av_done, u - 2)
                        nc.vector.tensor_copy(PT[:, u % 3, 0:512], PS[:, 4, :]).then_inc(pA_ready, 1)
                        if u % NH == NH - 1:
                            j = u // NH
                            dve.wait_ge(av_done, u + 1)
                            nc.vector.tensor_copy(OT[:, j, 4:8, :],
                                                  PS[:, 7, :].rearrange("p (k n) -> p k n", k=4)).then_inc(oB_ready, 1)
                dve_n[0] = st.n

            @block.scalar
            def _(act):
                for s in range(HEADS + 3):
                    if s < HEADS:
                        j, h = s // NH, s % NH
                        w = len(span(j)) * P
                        act.wait_ge(neg_ready, s + 1)
                        nc.scalar.activation(SS[:, s % 5, 0:w], SS[:, s % 5, 0:w], ACT.Exp, bias=nmx[:, s:s + 1],
                                             accum_out=rsum[:, s:s + 1]).then_inc(exp_done, 1)
                        nc.scalar.activation(esk[:, s:s + 1], nmx[:, s:s + 1], ACT.Exp,
                                             bias=sinkb[:, h:h + 1]).then_inc(sink_exp, 1)
                    u = s - 3
                    if 0 <= u < HEADS:
                        act.wait_ge(p_turned, u + 1)
                        if u >= 3:
                            act.wait_ge(av_done, u - 2)
                        if len(span(u // NH)) == 5:
                            nc.scalar.activation(PT[:, u % 3, 512:640], PS[:, 5, 0:P], ACT.Copy).then_inc(pB_ready, 1)
                        else:
                            act.sem_inc(pB_ready, 1)
                        if u % NH == NH - 1:
                            j = u // NH
                            act.wait_ge(av_done, u + 1)
                            nc.scalar.activation(OT[:, j, 0:4, :], PS[:, 6, :].rearrange("p (k n) -> p k n", k=4),
                                                 ACT.Copy).then_inc(oA_ready, 1)

            @block.gpsimd
            def _(pool):
                for s in range(HEADS):
                    w = len(span(s // NH)) * P
                    pool.wait_ge(total_inv, s + 1)
                    pool.tensor_scalar(SS[:, s % 5, 0:w], SS[:, s % 5, 0:w], esk[:, s:s + 1], None,
                                       ALU.mult).then_inc(p_normed, 1)

        def wait1(pe, k):
            if k == 0:
                pe.wait_ge(w_in[1], 32)
                pe.wait_ge(oA_ready, LT)
                pe.wait_ge(oB_ready, LT)

        lat = list(range(CT, TILES))
        with nc.Block() as block:
            project_and_route(block, 1, lambda i, k: OT[:, i, k, :], lambda k: WO[k // 4][:, k % 4, :], None, lat, wait1)
        moe_blocks(1)

        with nc.Block() as block:
            @block.gpsimd
            def _(pool):
                combine_pool(pool, 1, lat)

            @block.vector
            def _(dve):
                def store_ready(i):
                    t = lat[i]
                    nc.vector.scalar_tensor_tensor(out=X[:, t, :], in0=X[:, t, :], scalar=rstd[:, t:t + 1],
                                                   in1=ROWS[:, 0, :], op0=ALU.mult, op1=ALU.mult).then_inc(scaled, 1)

                combine_dve(dve, 1, lat, LT, store_ready, lambda i: None)

            @block.scalar
            def _(act):
                combine_act(act, 1, lat, LT, lambda i: None)

            @block.sync
            def _(sp):
                o = out[0].rearrange("(t p) d -> t p d", p=P)
                for i, t in enumerate(lat):
                    sp.wait_ge(scaled, KT + i + 1)
                    sp.dma_start(o[i], X[:, t, :]).then_inc(out_sem, 16)
                sp.wait_ge(out_sem, 16 * LT)


NAMES = ["x", "c", "ctx", "c_ctx", "w_mod", "b_mod", "norm_mix", "norm_ffn", "norm_f", "conv_pw1", "conv_pw1_b",
         "conv_dw", "conv_dw_b", "conv_ln_g", "conv_ln_b", "conv_pw2", "conv_pw2_b", "attn_w_qkv", "attn_w_o",
         "attn_sink", "moe_w_router", "moe_router_bias", "moe_w1", "moe_w3", "moe_w2"]


def kernel(**inputs):
    import concourse.bacc as bacc
    from concourse.bass_utils import run_bass_kernel_spmd

    nc = bacc.Bacc("TRN2", target_bir_lowering=False, num_devices=1)
    arrays, args = {}, {}
    for name in NAMES + ["consts"]:
        v = constant_table() if name == "consts" else np.ascontiguousarray(inputs[name])
        arrays[f"in_{name}"] = v
        args[name] = nc.dram_tensor(f"in_{name}", v.shape, mybir.dt.from_np(v.dtype), kind="ExternalInput").ap()
    out = nc.dram_tensor("out_0", (1, SEQ, D), F32, kind="ExternalOutput").ap()
    build(nc, args, out)
    r = run_bass_kernel_spmd(nc, [arrays], core_ids=[0])
    return r.results[0]["out_0"]
```
